# Optimizing a Trainium2 kernel written in Bass

```python
import jax, jax.numpy as jnp
from jax import lax
import numpy as np
import math

D_MODEL = 1024
BATCH = 1
SEQ = 256
DEPTH = 2

N_MIXERS = 2
N_ATTN_LAYERS = (DEPTH + 1) // 2
N_POOL_LAYERS = DEPTH // 2
N_HEADS = 16
QK_NOPE_DIM = 64
QK_ROPE_DIM = 32
V_HEAD_DIM = 64
Q_LORA_RANK = 256
KV_LORA_RANK = 128
ROPE_THETA = 10000.0
Q_BLOCK = 128
POOL_WINDOWS = (2, 4, 8, 16)
N_POOL_GROUPS = 4
POOL_GROUP_DIM = D_MODEL // N_POOL_GROUPS
N_EXPERT_GROUPS = 8
EXPERTS_PER_GROUP = 8
N_EXPERTS = N_EXPERT_GROUPS * EXPERTS_PER_GROUP
TOP_K_IN_GROUP = 2
D_EXPERT = 256
EXPERT_BLOCK = 128
DEEPNORM_ALPHA = (2 * DEPTH) ** 0.25
DEEPNORM_BETA = (8 * DEPTH) ** -0.25
LN_EPS = 1e-5
RMS_EPS = 1e-6


def layer_norm(x, g, b):
    xf = x.astype(jnp.float32)
    mu = jnp.mean(xf, axis=-1, keepdims=True)
    var = jnp.mean(jnp.square(xf - mu), axis=-1, keepdims=True)
    y = (xf - mu) * lax.rsqrt(var + LN_EPS) * g.astype(jnp.float32) + b.astype(jnp.float32)
    return y.astype(x.dtype)

def rms_norm(x, g):
    xf = x.astype(jnp.float32)
    y = xf * lax.rsqrt(jnp.mean(jnp.square(xf), axis=-1, keepdims=True) + RMS_EPS)
    return (y * g.astype(jnp.float32)).astype(x.dtype)

def rope_tables(positions):
    inv_freq = ROPE_THETA ** (-jnp.arange(0, QK_ROPE_DIM, 2, dtype=jnp.float32) / QK_ROPE_DIM)
    ang = positions.astype(jnp.float32)[..., None] * inv_freq
    return jnp.cos(ang), jnp.sin(ang)

def apply_rope(x, cos, sin):
    xf = x.astype(jnp.float32)
    half = xf.shape[-1] // 2
    x1, x2 = xf[..., :half], xf[..., half:]
    y = jnp.concatenate([x1 * cos - x2 * sin, x2 * cos + x1 * sin], axis=-1)
    return y.astype(x.dtype)

def mla_mixer(x, cos, sin, w_in, q_norm, w_uq, kv_norm, w_ukv, w_o):
    B, S, _ = x.shape
    lat = x @ w_in
    c_q = rms_norm(lat[..., :Q_LORA_RANK], q_norm)
    c_kv = rms_norm(lat[..., Q_LORA_RANK:Q_LORA_RANK + KV_LORA_RANK], kv_norm)
    k_rope = apply_rope(lat[..., Q_LORA_RANK + KV_LORA_RANK:], cos, sin)
    q = (c_q @ w_uq).reshape(B, S, N_HEADS, QK_NOPE_DIM + QK_ROPE_DIM)
    q_nope = q[..., :QK_NOPE_DIM]
    q_rope = apply_rope(q[..., QK_NOPE_DIM:], cos[:, :, None, :], sin[:, :, None, :])
    kv = (c_kv @ w_ukv).reshape(B, S, N_HEADS, QK_NOPE_DIM + V_HEAD_DIM)
    k_nope, v = kv[..., :QK_NOPE_DIM], kv[..., QK_NOPE_DIM:]
    scale = (QK_NOPE_DIM + QK_ROPE_DIM) ** -0.5
    outs = []
    for qs in range(0, S, Q_BLOCK):
        qe = qs + Q_BLOCK
        s = (jnp.einsum('bqhd,bkhd->bhqk', q_nope[:, qs:qe], k_nope[:, :qe],
                        preferred_element_type=jnp.float32)
             + jnp.einsum('bqhr,bkr->bhqk', q_rope[:, qs:qe], k_rope[:, :qe],
                          preferred_element_type=jnp.float32)) * scale
        causal = jnp.arange(qe)[None, :] <= jnp.arange(qs, qe)[:, None]
        s = jnp.where(causal, s, -jnp.inf)
        p = jax.nn.softmax(s, axis=-1).astype(v.dtype)
        outs.append(jnp.einsum('bhqk,bkhd->bqhd', p, v[:, :qe]))
    o = jnp.concatenate(outs, axis=1).reshape(B, S, N_HEADS * V_HEAD_DIM)
    return o @ w_o

def pool_mixer(x, w, b, scale):
    B, S, D = x.shape
    xf = x.astype(jnp.float32)
    cs = jnp.concatenate([jnp.zeros((B, 1, D), jnp.float32), jnp.cumsum(xf, axis=1)], axis=1)
    t = jnp.arange(S)
    means = []
    for gi, win in enumerate(POOL_WINDOWS):
        sl = slice(gi * POOL_GROUP_DIM, (gi + 1) * POOL_GROUP_DIM)
        hi = cs[:, 1:, sl]
        lo = cs[:, jnp.maximum(t + 1 - win, 0), sl]
        cnt = jnp.minimum(t + 1, win).astype(jnp.float32)[:, None]
        means.append((hi - lo) / cnt)
    pooled = jnp.concatenate(means, axis=-1) - xf
    y = jnp.einsum('bsgc,gcd->bsgd', pooled.reshape(B, S, N_POOL_GROUPS, POOL_GROUP_DIM),
                   w.astype(jnp.float32)).reshape(B, S, D) + b.astype(jnp.float32)
    return (y * scale.astype(jnp.float32)).astype(x.dtype)

def hier_moe(h, w_grp, b_grp, w_exp, b_exp, w1, w3, w2):
    B, S, D = h.shape
    tok = h.reshape(-1, D)
    N = tok.shape[0]
    hf = tok.astype(jnp.float32)
    g_logits = hf @ w_grp.astype(jnp.float32) + b_grp.astype(jnp.float32)
    g_prob = jax.nn.softmax(g_logits, axis=-1)
    g_sel = jnp.argmax(g_logits, axis=-1)
    g_gate = jnp.take_along_axis(g_prob, g_sel[:, None], axis=-1)
    e_logits = (hf @ w_exp.astype(jnp.float32) + b_exp.astype(jnp.float32)).reshape(N, N_EXPERT_GROUPS, EXPERTS_PER_GROUP)
    e_logits = jnp.take_along_axis(e_logits, g_sel[:, None, None], axis=1)[:, 0]
    e_prob = jax.nn.softmax(e_logits, axis=-1)
    top_p, top_i = lax.top_k(e_prob, TOP_K_IN_GROUP)
    gate = g_gate * top_p / jnp.sum(top_p, axis=-1, keepdims=True)
    expert = g_sel[:, None] * EXPERTS_PER_GROUP + top_i
    A = N * TOP_K_IN_GROUP
    flat_e = expert.reshape(-1).astype(jnp.int32)
    flat_tok = jnp.repeat(jnp.arange(N, dtype=jnp.int32), TOP_K_IN_GROUP)
    flat_gate = gate.reshape(-1)
    order = jnp.argsort(flat_e)
    e_sorted, tok_sorted, gate_sorted = flat_e[order], flat_tok[order], flat_gate[order]
    counts = jnp.bincount(flat_e, length=N_EXPERTS)
    padded = (counts + EXPERT_BLOCK - 1) // EXPERT_BLOCK * EXPERT_BLOCK
    start = jnp.cumsum(counts) - counts
    pend = jnp.cumsum(padded)
    pstart = pend - padded
    dest = pstart[e_sorted] + (jnp.arange(A, dtype=jnp.int32) - start[e_sorted])
    n_blocks = (A + N_EXPERTS * (EXPERT_BLOCK - 1) + EXPERT_BLOCK - 1) // EXPERT_BLOCK
    rows = jnp.zeros((n_blocks * EXPERT_BLOCK, D), tok.dtype).at[dest].set(tok[tok_sorted])
    blk_e = jnp.minimum(jnp.searchsorted(pend, jnp.arange(n_blocks) * EXPERT_BLOCK, side='right'), N_EXPERTS - 1)

    def expert_block(args):
        xb, e = args
        hb = jax.nn.silu(xb @ w1[e]) * (xb @ w3[e])
        return hb @ w2[e]

    y_rows = lax.map(expert_block, (rows.reshape(n_blocks, EXPERT_BLOCK, D), blk_e)).reshape(-1, D)
    y = y_rows[dest].astype(jnp.float32) * gate_sorted[:, None]
    out = jnp.zeros((N, D), jnp.float32).at[tok_sorted].add(y)
    return out.reshape(B, S, D).astype(h.dtype)

def first_inputs(seed: int = 0) -> dict:
    key = jax.random.key(seed)
    ks = jax.random.split(key, 24)
    f32 = jnp.float32
    nrm = lambda k, shape, s: jax.random.normal(k, shape, f32) * s
    LAT = Q_LORA_RANK + KV_LORA_RANK + QK_ROPE_DIM
    return {
        'x': jax.random.normal(ks[0], (BATCH, SEQ, D_MODEL), f32),
        'positions': (jnp.arange(SEQ, dtype=jnp.int32)[None, :]
                      + jax.random.randint(ks[1], (BATCH, 1), 0, 4096, dtype=jnp.int32)),
        'ln_g': 1.0 + nrm(ks[2], (DEPTH, 2, D_MODEL), 0.02),
        'ln_b': nrm(ks[3], (DEPTH, 2, D_MODEL), 0.02),
        'mla_w_in': nrm(ks[4], (N_ATTN_LAYERS, D_MODEL, LAT), D_MODEL ** -0.5),
        'mla_q_norm': 1.0 + nrm(ks[5], (N_ATTN_LAYERS, Q_LORA_RANK), 0.02),
        'mla_w_uq': nrm(ks[6], (N_ATTN_LAYERS, Q_LORA_RANK, N_HEADS * (QK_NOPE_DIM + QK_ROPE_DIM)), Q_LORA_RANK ** -0.5),
        'mla_kv_norm': 1.0 + nrm(ks[7], (N_ATTN_LAYERS, KV_LORA_RANK), 0.02),
        'mla_w_ukv': nrm(ks[8], (N_ATTN_LAYERS, KV_LORA_RANK, N_HEADS * (QK_NOPE_DIM + V_HEAD_DIM)), KV_LORA_RANK ** -0.5),
        'mla_w_o': nrm(ks[9], (N_ATTN_LAYERS, N_HEADS * V_HEAD_DIM, D_MODEL), (N_HEADS * V_HEAD_DIM) ** -0.5 * DEEPNORM_BETA),
        'pool_w': nrm(ks[10], (N_POOL_LAYERS, N_POOL_GROUPS, POOL_GROUP_DIM, POOL_GROUP_DIM), POOL_GROUP_DIM ** -0.5 * DEEPNORM_BETA),
        'pool_b': nrm(ks[11], (N_POOL_LAYERS, D_MODEL), 0.02),
        'pool_scale': 1.0 + nrm(ks[12], (N_POOL_LAYERS, D_MODEL), 0.1),
        'moe_w_grp': nrm(ks[13], (DEPTH, D_MODEL, N_EXPERT_GROUPS), D_MODEL ** -0.5),
        'moe_b_grp': nrm(ks[14], (DEPTH, N_EXPERT_GROUPS), 0.01),
        'moe_w_exp': nrm(ks[15], (DEPTH, D_MODEL, N_EXPERTS), D_MODEL ** -0.5),
        'moe_b_exp': nrm(ks[16], (DEPTH, N_EXPERTS), 0.01),
        'moe_w1': nrm(ks[17], (DEPTH, N_EXPERTS, D_MODEL, D_EXPERT), D_MODEL ** -0.5),
        'moe_w3': nrm(ks[18], (DEPTH, N_EXPERTS, D_MODEL, D_EXPERT), D_MODEL ** -0.5),
        'moe_w2': nrm(ks[19], (DEPTH, N_EXPERTS, D_EXPERT, D_MODEL), D_EXPERT ** -0.5 * DEEPNORM_BETA),
    }

def first_block(x, positions, ln_g, ln_b, mla_w_in, mla_q_norm, mla_w_uq, mla_kv_norm, mla_w_ukv, mla_w_o,
              pool_w, pool_b, pool_scale, moe_w_grp, moe_b_grp, moe_w_exp, moe_b_exp, moe_w1, moe_w3, moe_w2):
    cos, sin = rope_tables(positions)
    for i in range(DEPTH):
        j = i // N_MIXERS
        if i % N_MIXERS == 0:
            f = mla_mixer(x, cos, sin, mla_w_in[j], mla_q_norm[j], mla_w_uq[j],
                          mla_kv_norm[j], mla_w_ukv[j], mla_w_o[j])
        else:
            f = pool_mixer(x, pool_w[j], pool_b[j], pool_scale[j])
        x = layer_norm(DEEPNORM_ALPHA * x + f, ln_g[i, 0], ln_b[i, 0])
        f = hier_moe(x, moe_w_grp[i], moe_b_grp[i], moe_w_exp[i], moe_b_exp[i],
                     moe_w1[i], moe_w3[i], moe_w2[i])
        x = layer_norm(DEEPNORM_ALPHA * x + f, ln_g[i, 1], ln_b[i, 1])
    return x


N_MEM = 256
EPS = 1e-6
NEG_INF = -1e30

DIFF_HEADS = 8
DIFF_QK_DIM = 64
DIFF_V_DIM = 2 * DIFF_QK_DIM
DIFF_QK_WIDTH = 2 * DIFF_HEADS * DIFF_QK_DIM
DIFF_WIDTH = DIFF_HEADS * DIFF_V_DIM

DIL_GROUPS = ((128, 1), (512, 4), (2048, 16))
N_DIL_GROUPS = len(DIL_GROUPS)
DIL_HEADS = 4
DIL_HEAD_DIM = 128
DIL_WIDTH = DIL_HEADS * DIL_HEAD_DIM
DIL_QKV_WIDTH = N_DIL_GROUPS * DIL_WIDTH

MEM_HEADS = 4
MEM_HEAD_DIM = 128
MEM_WIDTH = MEM_HEADS * MEM_HEAD_DIM

N_BRANCH = 3

REL_BUCKETS = 32
REL_MAX_DIST = 1024
N_BIAS_HEADS = DIFF_HEADS + N_DIL_GROUPS * DIL_HEADS

IN_SIZES = (DIFF_QK_WIDTH, DIFF_QK_WIDTH, DIFF_WIDTH, DIFF_WIDTH,
            DIL_QKV_WIDTH, DIL_QKV_WIDTH, DIL_QKV_WIDTH, DIL_WIDTH,
            MEM_WIDTH, MEM_WIDTH, N_BRANCH * D_MODEL)
N_IN = sum(IN_SIZES)


def rmsnorm(x, g=None):
    xf = x.astype(jnp.float32)
    y = xf * lax.rsqrt(jnp.mean(xf * xf, axis=-1, keepdims=True) + EPS)
    if g is not None:
        y = y * g.astype(jnp.float32)
    return y.astype(x.dtype)

def t5_bucket(rel):
    half = REL_BUCKETS // 2
    max_exact = half // 2
    ret = jnp.where(rel > 0, half, 0)
    n = jnp.abs(rel)
    nf = jnp.maximum(n, 1).astype(jnp.float32)
    large = max_exact + (jnp.log(nf / max_exact) / math.log(REL_MAX_DIST / max_exact)
                         * (half - max_exact)).astype(jnp.int32)
    large = jnp.minimum(large, half - 1)
    return ret + jnp.where(n < max_exact, n, large)

def diff_attention(q, k, v, lam, bias_tab):
    B, S = q.shape[0], q.shape[1]
    nq = S // Q_BLOCK
    scale = DIFF_QK_DIM ** -0.5
    qb = q.reshape(B, nq, Q_BLOCK, 2, DIFF_HEADS, DIFF_QK_DIM).transpose(1, 0, 2, 3, 4, 5)
    kpos = jnp.arange(S, dtype=jnp.int32)

    def one_block(args):
        qblk, i = args
        qpos = i * Q_BLOCK + jnp.arange(Q_BLOCK, dtype=jnp.int32)
        bias = bias_tab[t5_bucket(kpos[None, :] - qpos[:, None])]
        bias = jnp.transpose(bias, (2, 0, 1)).astype(jnp.float32)
        s = jnp.einsum('bqmhd,bkmhd->bmhqk', qblk, k,
                       preferred_element_type=jnp.float32) * scale + bias
        p = jax.nn.softmax(s, axis=-1)
        w = p[:, 0] - lam * p[:, 1]
        return jnp.einsum('bhqk,bkhe->bqhe', w.astype(v.dtype), v)

    out = lax.map(one_block, (qb, jnp.arange(nq, dtype=jnp.int32)))
    return out.transpose(1, 0, 2, 3, 4).reshape(B, S, DIFF_HEADS, DIFF_V_DIM)

def dilated_group(q, k, v, window, dilation, bias_tab):
    B, S, H, dh = q.shape
    r = dilation
    half = window // (2 * r)
    nb = half
    L = S // r
    nblk = -(-L // nb)
    Lp = nblk * nb
    Bn = B * r
    scale = dh ** -0.5

    def to_strided(t):
        return t.reshape(B, L, r, H, dh).transpose(0, 2, 1, 3, 4).reshape(Bn, L, H, dh)

    def band(t):
        tp = jnp.pad(t, ((0, 0), (nb, Lp - L + nb), (0, 0), (0, 0)))
        tp = tp.reshape(Bn, nblk + 2, nb, H, dh)
        return jnp.concatenate([tp[:, :-2], tp[:, 1:-1], tp[:, 2:]], axis=2)

    qs = jnp.pad(to_strided(q), ((0, 0), (0, Lp - L), (0, 0), (0, 0))).reshape(Bn, nblk, nb, H, dh)
    kb = band(to_strided(k))
    vb = band(to_strided(v))

    qi = jnp.arange(nb, dtype=jnp.int32)
    kj = jnp.arange(3 * nb, dtype=jnp.int32) - nb
    delta = kj[None, :] - qi[:, None]
    ksub = jnp.arange(nblk, dtype=jnp.int32)[:, None] * nb + kj[None, :]
    valid = (jnp.abs(delta) <= half)[None, :, :] & ((ksub >= 0) & (ksub < L))[:, None, :]
    bias = bias_tab[t5_bucket(delta * r)].astype(jnp.float32).transpose(2, 0, 1)

    s = jnp.einsum('bnqhd,bnkhd->bnhqk', qs, kb,
                   preferred_element_type=jnp.float32) * scale + bias
    s = jnp.where(valid[None, :, None], s, NEG_INF)
    m = jnp.max(s, axis=-1, keepdims=True)
    e = jnp.exp(s - m)
    den = jnp.sum(e, axis=-1, keepdims=True)
    o = jnp.einsum('bnhqk,bnkhd->bnqhd', (e / den).astype(v.dtype), vb)
    lse = (m + jnp.log(den))[..., 0]

    o = o.reshape(Bn, Lp, H, dh)[:, :L]
    lse = lse.transpose(0, 1, 3, 2).reshape(Bn, Lp, H)[:, :L]
    o = o.reshape(B, r, L, H, dh).transpose(0, 2, 1, 3, 4).reshape(B, S, H, dh)
    lse = lse.reshape(B, r, L, H).transpose(0, 2, 1, 3).reshape(B, S, H)
    return o, lse

def memory_attention(q, mk, mv):
    s = jnp.einsum('bshd,bmhd->bhsm', q, mk,
                   preferred_element_type=jnp.float32) * (MEM_HEAD_DIM ** -0.5)
    p = jax.nn.softmax(s, axis=-1)
    return jnp.einsum('bhsm,bmhd->bshd', p.astype(mv.dtype), mv)

def mixer_layer(x, mem, layer_idx, g_norm, w_in, lam_p, w_mem_kv, g_mem,
                w_br_diff, w_br_dil, w_br_mem, w_out, rel_bias):
    B, S, _ = x.shape
    h = rmsnorm(x, g_norm)
    z = jnp.einsum('bsd,dn->bsn', h, w_in)
    splits = np.cumsum(IN_SIZES)[:-1].tolist()
    dq, dk, dv, dg, lq, lk, lv, lg, mq, mg, mgate = jnp.split(z, splits, axis=-1)

    lam_init = 0.8 - 0.6 * math.exp(-0.3 * layer_idx)
    lp = lam_p.astype(jnp.float32)
    lam = jnp.exp(jnp.dot(lp[0], lp[1])) - jnp.exp(jnp.dot(lp[2], lp[3])) + lam_init
    o_a = diff_attention(dq.reshape(B, S, 2, DIFF_HEADS, DIFF_QK_DIM),
                         dk.reshape(B, S, 2, DIFF_HEADS, DIFF_QK_DIM),
                         dv.reshape(B, S, DIFF_HEADS, DIFF_V_DIM),
                         lam, rel_bias[:, :DIFF_HEADS])
    o_a = rmsnorm(o_a) * (1.0 - lam_init)
    y_a = jnp.einsum('bse,ed->bsd', o_a.reshape(B, S, DIFF_WIDTH) * jax.nn.silu(dg), w_br_diff)

    lq = lq.reshape(B, S, N_DIL_GROUPS, DIL_HEADS, DIL_HEAD_DIM)
    lk = lk.reshape(B, S, N_DIL_GROUPS, DIL_HEADS, DIL_HEAD_DIM)
    lv = lv.reshape(B, S, N_DIL_GROUPS, DIL_HEADS, DIL_HEAD_DIM)
    outs, lses = [], []
    for g, (window, dilation) in enumerate(DIL_GROUPS):
        c0 = DIFF_HEADS + g * DIL_HEADS
        o_g, lse_g = dilated_group(lq[:, :, g], lk[:, :, g], lv[:, :, g], window, dilation,
                                   rel_bias[:, c0:c0 + DIL_HEADS])
        outs.append(o_g.astype(jnp.float32))
        lses.append(lse_g)
    wts = jax.nn.softmax(jnp.stack(lses, axis=0), axis=0)
    o_b = jnp.einsum('gbsh,gbshe->bshe', wts, jnp.stack(outs, axis=0)).astype(x.dtype)
    y_b = jnp.einsum('bse,ed->bsd', o_b.reshape(B, S, DIL_WIDTH) * jax.nn.silu(lg), w_br_dil)

    mem_n = rmsnorm(mem, g_mem)
    kv = jnp.einsum('bmd,dn->bmn', mem_n, w_mem_kv).reshape(B, mem.shape[1], 2, MEM_HEADS, MEM_HEAD_DIM)
    o_m = memory_attention(mq.reshape(B, S, MEM_HEADS, MEM_HEAD_DIM), kv[:, :, 0], kv[:, :, 1])
    y_m = jnp.einsum('bse,ed->bsd', o_m.reshape(B, S, MEM_WIDTH) * jax.nn.silu(mg), w_br_mem)

    gates = jax.nn.sigmoid(mgate).reshape(B, S, N_BRANCH, D_MODEL)
    merged = gates[:, :, 0] * y_a + gates[:, :, 1] * y_b + gates[:, :, 2] * y_m
    return x + jnp.einsum('bsd,de->bse', merged, w_out)

def second_inputs(seed: int = 0) -> dict:
    key = jax.random.key(seed)
    ks = jax.random.split(key, 14)
    f32 = jnp.float32
    nrm = jax.random.normal
    return {
        'x': nrm(ks[0], (BATCH, SEQ, D_MODEL), f32),
        'mem': nrm(ks[1], (BATCH, N_MEM, D_MODEL), f32),
        'g_norm': 1.0 + 0.02 * nrm(ks[2], (DEPTH, D_MODEL), f32),
        'w_in': nrm(ks[3], (DEPTH, D_MODEL, N_IN), f32) * D_MODEL ** -0.5,
        'diff_lambda': 0.1 * nrm(ks[4], (DEPTH, 4, DIFF_QK_DIM), f32),
        'w_mem_kv': nrm(ks[5], (DEPTH, D_MODEL, 2 * MEM_WIDTH), f32) * D_MODEL ** -0.5,
        'g_mem': 1.0 + 0.02 * nrm(ks[6], (DEPTH, D_MODEL), f32),
        'w_br_diff': nrm(ks[7], (DEPTH, DIFF_WIDTH, D_MODEL), f32) * DIFF_WIDTH ** -0.5,
        'w_br_dil': nrm(ks[8], (DEPTH, DIL_WIDTH, D_MODEL), f32) * DIL_WIDTH ** -0.5,
        'w_br_mem': nrm(ks[9], (DEPTH, MEM_WIDTH, D_MODEL), f32) * MEM_WIDTH ** -0.5,
        'w_out': nrm(ks[10], (DEPTH, D_MODEL, D_MODEL), f32) * D_MODEL ** -0.5,
        'rel_bias': 0.2 * nrm(ks[11], (REL_BUCKETS, N_BIAS_HEADS), f32),
        'g_final': 1.0 + 0.02 * nrm(ks[12], (D_MODEL,), f32),
    }

def second_block(x, mem, g_norm, w_in, diff_lambda, w_mem_kv, g_mem,
              w_br_diff, w_br_dil, w_br_mem, w_out, rel_bias, g_final):
    for l in range(DEPTH):
        x = mixer_layer(x, mem, l, g_norm[l], w_in[l], diff_lambda[l], w_mem_kv[l], g_mem[l],
                        w_br_diff[l], w_br_dil[l], w_br_mem[l], w_out[l], rel_bias)
    return rmsnorm(x, g_final)


def setup_inputs(seed=0):
    out = dict(first_inputs(seed))
    for name, value in second_inputs(seed + 1).items():
        if name != "x":
            out[name + "_2"] = value
    return out


def reference(
    x, positions, ln_g, ln_b, mla_w_in, mla_q_norm, mla_w_uq, mla_kv_norm, mla_w_ukv, mla_w_o,
    pool_w, pool_b, pool_scale, moe_w_grp, moe_b_grp, moe_w_exp, moe_b_exp, moe_w1, moe_w3,
    moe_w2, mem_2, g_norm_2, w_in_2, diff_lambda_2, w_mem_kv_2, g_mem_2, w_br_diff_2,
    w_br_dil_2, w_br_mem_2, w_out_2, rel_bias_2, g_final_2,
):
    x = first_block(
        x, positions, ln_g, ln_b, mla_w_in, mla_q_norm, mla_w_uq, mla_kv_norm, mla_w_ukv,
        mla_w_o, pool_w, pool_b, pool_scale, moe_w_grp, moe_b_grp, moe_w_exp, moe_b_exp, moe_w1,
        moe_w3, moe_w2,
    )
    return second_block(
        x, mem_2, g_norm_2, w_in_2, diff_lambda_2, w_mem_kv_2, g_mem_2, w_br_diff_2, w_br_dil_2,
        w_br_mem_2, w_out_2, rel_bias_2, g_final_2,
    )


_drawn_inputs = setup_inputs


def setup_inputs(seed=0):
    import zlib

    import numpy as np

    out = dict(_drawn_inputs(seed))
    spreads = {}
    factors = {'mla_q_norm': 8.0,
     'mla_kv_norm': 8.0,
     'moe_b_grp': 8.0,
     'moe_b_exp': 8.0,
     'g_norm_2': 4.153,
     'diff_lambda_2': 2.995,
     'g_mem_2': 8.0,
     'g_final_2': 2.835}
    for name, (base, spread) in spreads.items():
        noise = np.random.default_rng([zlib.crc32(name.encode()), seed]).standard_normal(out[name].shape)
        drawn = base * np.exp(spread * noise) if base else spread * noise
        out[name] = __import__('jax').numpy.asarray(drawn.astype(out[name].dtype))
    for name, factor in factors.items():
        out[name] = (out[name] * factor).astype(out[name].dtype)
    return out
```

```python
from contextlib import ExitStack

import concourse.bass as bass
import numpy as np
from concourse import mybir

F32 = mybir.dt.float32
I32 = mybir.dt.int32
ALU = mybir.AluOpType
ACT = mybir.ActivationFunctionType
X = mybir.AxisListType.X

P = 128
T = 256
TT = T // P
D = 1024
KD = D // P
DEPTH = 2
ALPHA = (2 * DEPTH) ** 0.25
NEG = -1e30

QL, KVL, ROPE, NOPE, VD, NH = 256, 128, 32, 64, 64, 16
LAT = QL + KVL + ROPE
QH = NOPE + ROPE
RH = ROPE // 2
MLA_SCALE = QH ** -0.5
TWO_PI = 2 * np.pi
ROUND = 1.5 * 2.0 ** 23

NG, EG = 8, 8
NE = NG * EG
FE = 256
SL = 32
NS = 2 * T
XS = NS + SL
SWEEPS = T // SL
RINGS = 4
SLOT = 2 * KD * FE + FE // P * D
WINDOWS = (2, 4, 8, 16)
PG = D // len(WINDOWS)

DH, DQ, DV = 8, 64, 128
LG, LH, HD = 3, 4, 128
DILATION = (1, 4, 16)
MH = 4
CW = 512
CHUNK = KD * CW
CRINGS = 4
BUCKETS, BIASES = 32, DH + LG * LH
GAPS = 2 * T


def bias_constants():
    rel = np.arange(GAPS) - (T - 1)
    half, exact = BUCKETS // 2, BUCKETS // 4
    n = np.abs(rel)
    large = exact + (np.log(np.maximum(n, 1).astype(np.float32) / np.float32(exact)) / np.log(1024 / exact)
                     * (half - exact)).astype(np.int32)
    bucket = np.where(rel > 0, half, 0) + np.where(n < exact, n, np.minimum(large, half - 1))
    onehot = (np.arange(P)[:, None] == bucket[None, :]) * 1.0
    mask = np.zeros((P, GAPS))
    for g, r in enumerate(DILATION):
        seen = (n % r == 0) & (n // r <= 64)
        mask[DH + LH * g:DH + LH * (g + 1)] = np.where(seen, 0.0, NEG)
    return np.concatenate([mask, onehot], 1).astype(np.float32)


def layer_plan():
    w = [("w_in", c) for c in range(26)]
    plan = [(("mem_kv", 0), None, None), (("mem_kv", 1), None, None)]
    plan += [(w[c], None, None) for c in range(8)]
    plan += [(w[8 + h], ("diff", h), None) for h in range(8)]
    plan += [(w[16], None, None), (w[17], None, "diff")]
    plan += [(w[20], ("dil", 0), None), (("br_diff", 0), ("dil", 1), None), (w[21], ("dil", 2), None),
             (("br_diff", 1), ("dil", 3), None), (w[18], None, None), (w[19], None, "dil")]
    plan += [(w[22], ("mem", 0), None), (w[23], ("mem", 1), None), (("br_dil", 0), ("mem", 2), None),
             (w[24], ("mem", 3), None), (w[25], None, "mem"), (("br_mem", 0), None, "merged"),
             (("w_out", 0), None, None), (("w_out", 1), None, None)]
    return plan


PLAN = layer_plan()
HALVES = [4 if c[0] in ("br_dil", "br_mem") else 2 for c, _, _ in PLAN]
HALF0 = [sum(HALVES[:i]) for i in range(len(PLAN) + 1)]
NHALF = HALF0[-1]
JOBS = [j for _, j, _ in PLAN if j]
NJOB = len(JOBS)
MAPS = dict(diff=2, dil=LG, mem=1)
TURNS = dict(diff=1, dil=LG, mem=1)
JOB_SCALE = dict(diff=DQ ** -0.5, dil=HD ** -0.5, mem=HD ** -0.5)
TILES = dict(diff=KD, dil=LH, mem=MH, merged=KD)
LAM0 = [0.8 - 0.6 * float(np.exp(-0.3 * l)) for l in range(DEPTH)]


def chunk_of(name, c=0):
    return [p[0] for p in PLAN].index((name, c))


def turn_numbers():
    at, n = {"mem_x": 0, "h": 4}, 8
    for _, job, after in PLAN:
        if job:
            at[job] = n
            n += TURNS[job[0]]
        if after:
            at[after] = n
            n += TILES[after] // 2
    return at, n


TURN0, NTURN = turn_numbers()
CHAINED = 193


def shape_constants():
    p = np.arange(P)
    ident = np.eye(P)
    before = (p[:, None] < p[None, :]) * 1.0
    ones = np.ones((P, P))
    iota = np.broadcast_to(np.arange(NS), (P, NS))
    falling = np.broadcast_to(8.0 - np.arange(8), (P, 8))
    sweep_floor = np.broadcast_to(SL * np.arange(SWEEPS), (P, SWEEPS))
    q = np.arange(TT)[None, :, None] * P + p[:, None, None]
    causal = np.where(np.arange(T)[None, None, :] <= q, 0.0, NEG).reshape(P, TT * T)
    inv = (np.float32(10000.0) ** (-np.arange(0, ROPE, 2, dtype=np.float32) / np.float32(ROPE)))
    freq = np.broadcast_to(inv, (P, RH))
    small = np.concatenate([ident, before, ones, iota, falling, sweep_floor, causal, freq], 1)
    t = np.arange(T)
    band = np.zeros((P, len(WINDOWS), TT, T))
    for g, w in enumerate(WINDOWS):
        m = ((t[:, None] <= t[None, :]) & (t[:, None] > t[None, :] - w)) / np.minimum(t + 1, w)[None, :]
        m = m - np.eye(T)
        band[:, g] = m.reshape(TT, P, T).transpose(1, 0, 2)
    return small.astype(np.float32), band.reshape(P, -1).astype(np.float32)


PI_A = 6.28125
PI_B = float(np.float32(np.round((TWO_PI - PI_A) * 2.0 ** 22) / 2.0 ** 22))
PI_C = float(np.float32(TWO_PI - PI_A - PI_B))


def build(nc, a, out):
    ctx = ExitStack()
    with ctx:
        def sb(name, words, dt=F32):
            return ctx.enter_context(nc.sbuf_tensor(name, [P, words], dt))

        sems = {}

        def sem(name):
            if name not in sems:
                sems[name] = ctx.enter_context(nc.semaphore(name))
            return sems[name]

        ps = ctx.enter_context(nc.psum_tensor("ps", [P, 8, 512], F32))
        ring = sb("ring", RINGS * SLOT)
        x_tm = sb("x_tm", TT * D)[:, :].rearrange("p (t d) -> p t d", t=TT)
        xT = sb("xT", KD * T)[:, :].rearrange("p (k t) -> p k t", k=KD)
        consts = sb("consts", 3 * P + NS + 8 + SWEEPS + TT * T + RH)
        AW = 21888
        arena = sb("arena", AW)
        starts_i = sb("starts_i", SWEEPS * NE, I32)
        nsw_i = sb("nsw_i", 1, I32)
        pos_i = sb("pos_i", TT, I32)
        tiny = sb("tiny", 640)
        y_sorted = nc.dram_tensor("y_sorted", (XS, D), F32).ap()

        o = 0
        views = []
        for w in (P, P, P, NS, 8, SWEEPS, TT * T, RH):
            views.append(consts[:, o:o + w])
            o += w
        ident, before, ones, iota, falling, sweep_floor, causal, freq = views

        def carve(buf, start, *dims):
            n = int(np.prod(dims))
            v = buf[:, start:start + n]
            if len(dims) == 2:
                v = v.rearrange("p (a b) -> p a b", a=dims[0])
            if len(dims) == 3:
                v = v.rearrange("p (a b c) -> p a b c", a=dims[0], b=dims[1])
            return v

        def places(buf, start, end, *sizes):
            got, at = [], start
            for dims in sizes:
                got.append(carve(buf, at, *dims))
                at += int(np.prod(dims))
            assert at <= end, (at, end)
            return got

        def over(ap, axis, n):
            s = list(ap.shape)
            s.insert(axis, n)
            return ap.unsqueeze(axis).to_broadcast(s)

        win, wuq, wukv, qtm, kT, v_tm, lat, cT, S, PT, qg, kvg = places(
            arena, 0, AW, (KD, LAT), (TT, NH * QH), (2 * NH * NOPE,), (TT, NH + 1, QH), (NH, T), (TT, D), (TT, LAT),
            (3, T), (2, TT * T), (2, TT * T), (QL,), (KVL,))
        o_tm = carve(arena, 0, TT, D)
        o_T = carve(arena, TT * D, KD, T)
        gain = carve(arena, 2 * TT * D, D)
        shift = carve(arena, 2 * TT * D + D, D)
        r2 = 2 * SLOT
        wo, qT = places(ring, r2, RINGS * SLOT, (KD, D), (NH, T))
        w_slots = [carve(ring, s * SLOT, SLOT) for s in range(RINGS)]
        MO = 2 * TT * D + 2 * D
        (wr, br, lg, XsT, Pm, CT, C, xe, hA, sg, hT, yS, E1, E2, A, dst, cntT, tmp, stf) = places(
            arena, MO, AW, (KD, NG + NE), (NG + NE,), (TT, NG + NE), (KD, XS), (TT, NS),
            (TT, NS), (NS // P, T), (2, KD * SL), (2, P), (2, 2 * SL), (2, 2 * SL), (2, T), (TT, NE), (TT, NE),
            (TT, NE), (TT, NE), (P,), (TT, NS), (SWEEPS * NE,))
        Ys = carve(arena, 0, NS // P, D)
        _tiny = [0]

        def tiny_at(*dims):
            v = carve(tiny, _tiny[0], *dims)
            _tiny[0] += int(np.prod(dims))
            assert _tiny[0] <= 640
            return v

        ssq = tiny_at(TT, 2)
        ang = tiny_at(TT, RH)
        kk = tiny_at(2, TT * RH)
        rr = tiny_at(2, TT * RH)
        cs = tiny_at(2, TT * RH)
        posf = tiny_at(TT)
        nmx = tiny_at(2, TT)
        den = tiny_at(2, TT)
        rden = tiny_at(2, TT)
        gm, gx, gs, m1, m2, tx, rat, dn, g1, g2, d1, d2 = [tiny_at(TT) for _ in range(12)]
        geq, goh, es, eeq, o1, o2 = [tiny_at(TT, 8) for _ in range(6)]
        cmax = tiny_at(1)
        swf = tiny_at(SWEEPS)
        nswf = tiny_at(1)
        last = tiny_at(1)
        stats = tiny_at(TT, 2 * 6)
        agg = tiny_at(TT, 2)

        pool_places = places(arena, MO, AW, (KD, PG), (len(WINDOWS) * TT * T,), (D,), (D,))
        pool_y = carve(arena, MO + KD * PG + len(WINDOWS) * TT * T + 2 * D, TT, D)
        goh_e = tiny_at(TT, 8)
        vare, rt, rt2 = [tiny_at(4) for _ in range(3)]
        rope_tmp = carve(arena, 0, 4, (NH + 1) * RH)

        cslots = [carve(ring, s * CHUNK, KD, CW) for s in range(CRINGS)]
        cslots_wide = [carve(ring, s * CHUNK, KD // 2, D) for s in range(CRINGS)]
        tail = CRINGS * CHUNK
        bias, mkT, mv = places(ring, tail, RINGS * SLOT, (LG * LH, TT * T), (MH, T), (TT, MH * HD))
        ZB = KD * D + 0
        dqk, dv, dgt, lqk, lv, lgt, S3, PT3 = places(
            arena, 0, AW, (2 * KD, T), (TT, D), (TT, D), (2 * LG * LH, T), (TT, LG * LH * HD), (TT, LH * HD),
            (LG, TT * T), (LG, TT * T))
        oaT, mqT, mgt = places(arena, 0, 4096, (KD, T), (MH, T), (TT, MH * HD))
        gates = carve(arena, 4096, TT, D)
        merged = dgt
        h_tm, mem_tm, memT, g_x, g_m = places(arena, 8192, AW - 3072, (TT, D), (TT, D), (KD, T), (D,), (D,))
        obT, omT, mergedT = places(arena, 8192, 8192 + 6144, (LH, T), (MH, T), (KD, T))
        gate_of = dict(diff=dgt, dil=lgt, mem=mgt)
        turned_of = dict(diff=oaT, dil=obT, mem=omT, merged=mergedT)
        _tiny[0] = 0
        lam_in = carve(arena, 8192, DEPTH * 4, DQ)
        lam_prod = carve(arena, 8192 + 512, DEPTH * 2, DQ)
        lam_dot, lam_exp = tiny_at(DEPTH, 2), tiny_at(DEPTH, 2)
        lam_neg, lam_rest = tiny_at(DEPTH), tiny_at(DEPTH)
        ssq4 = tiny_at(4)
        ssq16 = tiny_at(DH, TT)
        nmx3, den3, rden3 = tiny_at(4), tiny_at(4), tiny_at(4)
        vare3, rt3, rt4 = tiny_at(16), tiny_at(16), tiny_at(16)
        assert _tiny[0] <= 320
        bias_mask, bias_onehot = S[:, 0, :], S[:, 1, :]
        rel_sb = PT[:, 0, 480:480 + BIASES]
        gap_bias = nc.dram_tensor("gap_bias", (BIASES, P, GAPS), F32).ap()

        block = ctx.enter_context(nc.Block())

        class Chain:

            def __init__(self, eng, name, base=0):
                self.eng, self.sem, self.n, self.base = eng, sem(name), 0, base

            def __call__(self, ins):
                self.n += 1
                ins.then_inc(self.sem, 1)
                self.eng.wait_ge(self.sem, self.base + self.n)


        def products(l, n):
            return (l + 1) * NHALF + n

        def wait_taken(eng, l, chunk):
            for b in range(2):
                eng.wait_ge(sem(f"bank_taken{b}"), l * (NHALF // 2) + HALF0[chunk + 1] // 2 + 1)

        def chunk_source(l, chunk):
            name, c = chunk
            cols = slice(c * CW, (c + 1) * CW)
            if name == "w_in":
                return a["w_in"][l, :, cols].rearrange("(p k) n -> p k n", k=KD)
            if name == "mem_kv":
                return a["w_mem_kv"][l, :, cols].rearrange("(p k) n -> p k n", k=KD)
            if name in ("br_diff", "w_out"):
                return a[name if name == "w_out" else "w_" + name][l, :, cols].rearrange("(k p) n -> p k n", p=P)
            return a["w_" + name][l].rearrange("(k p) n -> p k n", p=P)

        def sp_second(sp):
            with sp.Fori(0, DEPTH) as l:
                for i, (chunk, _, _) in enumerate(PLAN):
                    s = i % CRINGS
                    if i >= CRINGS:
                        sp.wait_ge(sem("bank_full"), products(l, HALF0[i - CRINGS + 1]))
                    else:
                        before_ = max(j for j in range(len(PLAN)) if j % CRINGS == s)
                        sp.wait_ge(sem("bank_full"), products(l, HALF0[before_ + 1] - NHALF))
                    dst = cslots_wide[s] if chunk[0] in ("br_dil", "br_mem") else cslots[s]
                    sp.dma_start(dst, chunk_source(l, chunk)).then_inc(sem(f"chunk_in{s}"), 16)

        def chunk_loads(s):
            return len([i for i in range(len(PLAN)) if i % CRINGS == s])

        def pe_second(pe):
            with pe.Fori(0, DEPTH) as l:
                turned = [0]

                def turn_tiles(pairs):
                    n = turned[0]
                    for bank in pairs:
                        pe.wait_ge(sem("turn_taken"), l * NTURN + n + 1)
                        for c, src in enumerate(bank):
                            i = nc.tensor.transpose(ps[:, 5 + n % 2, c * P:(c + 1) * P], src, ident)
                        i.then_inc(sem("turn_full"), 1)
                        n += 1
                    turned[0] = n

                pe.wait_ge(sem("normed"), l + 1)
                for src in (mem_tm, h_tm):
                    turn_tiles([[src[:, t, k::KD] for k in (2 * c, 2 * c + 1) for t in range(TT)] for c in range(4)])
                pe.wait_ge(sem("turn_read"), l * NTURN + 8)
                job_n = 0

                def scores(kind, h, J):
                    last = dict(diff=chunk_of("w_in", 3), dil=chunk_of("w_in", 17), mem=chunk_of("w_in", 19))[kind]
                    if h == 0:
                        wait_taken(pe, l, last)
                    pe.wait_ge(sem("s_taken2"), l * NJOB + J + 1)
                    for m in range(MAPS[kind]):
                        for t in range(TT):
                            tok = slice(t * P, (t + 1) * P)
                            if kind == "diff":
                                rows = slice(DQ * (h % 2), DQ * (h % 2) + DQ)
                                q = dqk[rows, 4 * m + h // 2, tok]
                                k = dqk[rows, KD + 4 * m + h // 2, :]
                            elif kind == "dil":
                                q = lqk[:, LH * m + h, tok]
                                k = lqk[:, LG * LH + LH * m + h, :]
                            else:
                                q, k = mqT[:, h, tok], mkT[:, h, :]
                            i = nc.tensor.matmul(ps[:, 2 + m, t * T:(t + 1) * T], q, k, start=True, stop=True)
                    i.then_inc(sem("s_full2"), 1)

                def turn(kind, h, J):
                    if kind == "diff":
                        pe.wait_ge(sem("w_ready2"), l * DH + h + 1)
                    else:
                        pe.wait_ge(sem("p_ready2"), l * NJOB + J + 1)
                    turn_tiles([[S3[:, m, t * T + k * P:t * T + (k + 1) * P] for k in range(2) for t in range(TT)]
                                for m in range(TURNS[kind])])

                def values(kind, h, J):
                    if kind == "diff" and h == 0:
                        wait_taken(pe, l, chunk_of("w_in", 5))
                    pe.wait_ge(sem("turn_read"), l * NTURN + turned[0])
                    pe.wait_ge(sem("o_taken2"), l * NJOB + J + 1)
                    n = TURNS[kind]
                    for t in range(TT):
                        for m in range(n):
                            for k in range(2):
                                if kind == "diff":
                                    v_ = dv[:, k, h * DV:(h + 1) * DV]
                                elif kind == "dil":
                                    v_ = lv[:, k, (LH * m + h) * HD:(LH * m + h + 1) * HD]
                                else:
                                    v_ = mv[:, k, h * HD:(h + 1) * HD]
                                i = nc.tensor.matmul(ps[:, 7, t * P:(t + 1) * P],
                                                     PT3[:, m, k * T + t * P:k * T + (t + 1) * P], v_,
                                                     start=(m == 0 and k == 0), stop=(m == n - 1 and k == 1))
                    i.then_inc(sem("o_full2"), 1)

                def product(i, half):
                    (name, c), s, n = PLAN[i][0], i % CRINGS, HALF0[i] + half
                    if half == 0:
                        pe.wait_ge(sem(f"chunk_in{s}"), (l * chunk_loads(s) + i // CRINGS + 1) * 16)
                    pe.wait_ge(sem(f"bank_taken{n % 2}"), l * (NHALF // 2) + n // 2 + 1)
                    bank = ps[:, n % 2, :]
                    w = cslots[s]
                    if name in ("w_in", "mem_kv") and ((name, c) == ("mem_kv", 0) or by_feature(name, c)):
                        x_ = memT if name == "mem_kv" else xT
                        for u in range(2):
                            f = 2 * half + u
                            for k in range(KD):
                                m = nc.tensor.matmul(bank[:, u * T:(u + 1) * T], w[:, k, f * P:(f + 1) * P], x_[:, k, :],
                                                     start=(k == 0), stop=(k == KD - 1))
                    elif name in ("br_dil", "br_mem"):
                        x_, w = (obT if name == "br_dil" else omT), cslots_wide[s]
                        t, cc = half // 2, half % 2
                        for k in range(KD // 2):
                            m = nc.tensor.matmul(bank, x_[:, k, t * P:(t + 1) * P], w[:, k, cc * CW:(cc + 1) * CW],
                                                 start=(k == 0), stop=(k == KD // 2 - 1))
                    else:
                        x_ = dict(w_in=xT, mem_kv=memT, br_diff=oaT, w_out=mergedT)[name]
                        for k in range(KD):
                            m = nc.tensor.matmul(bank, x_[:, k, half * P:(half + 1) * P], w[:, k, :],
                                                 start=(k == 0), stop=(k == KD - 1))
                    m.then_inc(sem("bank_full"), 1)

                for i, (chunk, job, after) in enumerate(PLAN):
                    if job:
                        scores(*job, job_n)
                    if chunk[0] in ("br_diff", "br_dil", "br_mem", "w_out"):
                        what = dict(br_diff="diff", br_dil="dil", br_mem="mem", w_out="merged")[chunk[0]]
                        pe.wait_ge(sem("turn_read"), l * NTURN + TURN0[what] + TILES[what] // 2)
                    product(i, 0)
                    if job:
                        turn(*job, job_n)
                    for half in range(1, HALVES[i]):
                        product(i, half)
                    if job:
                        values(*job, job_n)
                        job_n += 1
                    if after:
                        pe.wait_ge(sem(f"{after}_ready2"), l + 1)
                        src = merged if after == "merged" else gate_of[after]
                        turn_tiles([[src[:, t, k * P:(k + 1) * P] for k in (2 * c, 2 * c + 1) for t in range(TT)]
                                    for c in range(TILES[after] // 2)])
                assert turned[0] == NTURN and job_n == NJOB

        def by_feature(name, c):
            return name == "w_in" and (c < 4 or 8 <= c < 14 or c == 18)

        def act_second(act):
            with act.Fori(0, DEPTH) as l:
                act.wait_ge(sem("mem_in"), l * 16 + 16)
                act.wait_ge(sem("x_ready2"), l + 1)
                for n, src in enumerate((x_tm, mem_tm)):
                    for t in range(TT):
                        i = nc.scalar.activation(PT3.rearrange("p a b -> p (a b)")[:, 0:D], src[:, t, :], ACT.Square,
                                                 accum_out=ssq4[:, 2 * n + t:2 * n + t + 1])
                        i.then_inc(sem("ssq_each"), 1)
                        act.wait_ge(sem("ssq_each"), l * 4 + 2 * n + t + 1)
                act.sem_inc(sem("ssq_ready2"), 1)
                act_root2(act, l * 2 + 1, 4)
                turned = [0]

                def take_turned(dsts):
                    n = turned[0]
                    for dst in dsts:
                        act.wait_ge(sem("turn_full"), l * NTURN + n + 1)
                        src = ps[:, 5 + n % 2, :]
                        if len(dst.shape) == 3:
                            src = src.rearrange("p (a b) -> p a b", a=2)
                        nc.scalar.copy(dst, src).then_inc(sem("turn_read"), 1)
                        act.wait_ge(sem("turn_read"), l * NTURN + n + 1)
                        act.sem_inc(sem("turn_taken"), 1)
                        n += 1
                    turned[0] = n

                take_turned([memT[:, 2 * c:2 * c + 2, :] for c in range(4)])
                take_turned([xT[:, 2 * c:2 * c + 2, :] for c in range(4)])
                job_n = 0

                def exps(kind, h, J):
                    act.wait_ge(sem("max_ready2"), l * NJOB + J + 1)
                    if kind == "diff":
                        for m in range(2):
                            for t in range(TT):
                                part = S3[:, m, t * T:(t + 1) * T]
                                i = nc.scalar.activation(part, part, ACT.Exp, bias=nmx3[:, 2 * m + t:2 * m + t + 1],
                                                         accum_out=den3[:, 2 * m + t:2 * m + t + 1])
                    else:
                        for t in range(TT):
                            part = S3[:, 0:MAPS[kind], t * T:(t + 1) * T]
                            i = nc.scalar.activation(part, part, ACT.Exp, bias=nmx3[:, t:t + 1],
                                                     accum_out=den3[:, t:t + 1])
                    i.then_inc(sem("p_ready2"), 1)

                gate_n = [0]

                def take(i, half):
                    (name, c), n = PLAN[i][0], HALF0[i] + half
                    if name in ("br_diff", "br_dil", "br_mem", "w_out"):
                        return
                    act.wait_ge(sem("bank_full"), products(l, n + 1))
                    bank = ps[:, n % 2, :]
                    two = bank.rearrange("p (a b) -> p a b", a=2)
                    taken = sem(f"bank_taken{n % 2}")
                    if name == "mem_kv":
                        if c == 0:
                            nc.scalar.copy(mkT[:, 2 * half:2 * half + 2, :], two).then_inc(taken, 1)
                        else:
                            nc.scalar.copy(mv[:, half, :], bank).then_inc(taken, 1)
                    elif c < 4:
                        nc.scalar.copy(dqk[:, 4 * c + 2 * half:4 * c + 2 * half + 2, :], two).then_inc(taken, 1)
                    elif c < 6:
                        nc.scalar.copy(dv[:, half, (c - 4) * CW:(c - 3) * CW], bank).then_inc(taken, 1)
                    elif 8 <= c < 14:
                        f = 4 * (c - 8) + 2 * half
                        nc.scalar.copy(lqk[:, f:f + 2, :], two).then_inc(taken, 1)
                    elif 14 <= c < 17:
                        nc.scalar.copy(lv[:, half, (c - 14) * CW:(c - 13) * CW], bank).then_inc(taken, 1)
                    elif c == 18:
                        nc.scalar.copy(mqT[:, 2 * half:2 * half + 2, :], two).then_inc(taken, 1)
                    elif c >= 20:
                        if c in (22, 24) and half == 0:
                            wait_taken(act, l, chunk_of(*{22: ("br_diff", 1), 24: ("br_dil", 0)}[c]))
                        nc.scalar.activation(gates[:, half, (c % 2) * CW:(c % 2 + 1) * CW], bank, ACT.Tanh,
                                             scale=0.5).then_inc(taken, 1)
                    else:
                        g = dgt[:, half, (c - 6) * CW:(c - 5) * CW] if c < 8 else (lgt if c == 17 else mgt)[:, half, :]
                        nc.scalar.activation(g, bank, ACT.Tanh, scale=0.5).then_inc(sem("tanh_ready"), 1)

                for i, (chunk, job, after) in enumerate(PLAN):
                    if job:
                        exps(*job, job_n)
                    take(i, 0)
                    if job:
                        act.wait_ge(sem("o_full2"), l * NJOB + job_n + 1)
                        take_turned([PT3[:, m, :] for m in range(TURNS[job[0]])])
                    for half in range(1, HALVES[i]):
                        take(i, half)
                    if job:
                        if job[0] == "diff":
                            act.wait_ge(sem("o_full2"), l * NJOB + job_n + 2)
                            for t in range(TT):
                                n = nc.scalar.activation(PT3[:, 0, t * P:(t + 1) * P], ps[:, 7, t * P:(t + 1) * P],
                                                         ACT.Square, accum_out=ssq16[:, job[1], t:t + 1])
                            n.then_inc(sem("o_squared"), 1)
                            if job[1] == DH - 1:
                                act_root2(act, l * 2 + 2, 16)
                        job_n += 1
                    if after:
                        take_turned([turned_of[after][:, 2 * c:2 * c + 2, :] for c in range(TILES[after] // 2)])

        def act_root2(act, k, n):
            act.wait_ge(sem("var_ready2"), k)
            nc.scalar.activation(rt3[:, 0:n], vare3[:, 0:n], ACT.Sqrt).then_inc(sem("root_ready2"), 1)

        def inverse_root2(v, ch, var, n, eps, k):
            ch(nc.vector.tensor_scalar(vare3[:, 0:n], var, eps, None, ALU.add))
            v.sem_inc(sem("var_ready2"), 1)
            v.wait_ge(sem("root_ready2"), k)
            ch(nc.vector.reciprocal(rt3[:, 0:n], rt3[:, 0:n]))
            ch(nc.vector.tensor_tensor(rt4[:, 0:n], rt3[:, 0:n], rt3[:, 0:n], ALU.mult))
            ch(nc.vector.tensor_tensor(rt4[:, 0:n], rt4[:, 0:n], vare3[:, 0:n], ALU.mult))
            ch(nc.vector.tensor_scalar(rt4[:, 0:n], rt4[:, 0:n], -0.5, 1.5, ALU.mult, ALU.add))
            ch(nc.vector.tensor_tensor(var, rt3[:, 0:n], rt4[:, 0:n], ALU.mult))

        def dve_lambda(v, ch):
            v.wait_ge(sem("lam_in"), 16)
            pairs = lam_in.rearrange("p (a b) d -> p a b d", b=2)
            ch(nc.vector.tensor_tensor(lam_prod, pairs[:, :, 0, :], pairs[:, :, 1, :], ALU.mult))
            ch(nc.vector.tensor_reduce(lam_dot.rearrange("p a b -> p (a b)"), lam_prod, X, ALU.add))
            v.sem_inc(sem("lam_dots"), 1)
            v.wait_ge(sem("lam_exps"), 1)
            ch(nc.vector.tensor_tensor(lam_neg, lam_exp[:, :, 1], lam_exp[:, :, 0], ALU.subtract))
            for l in range(DEPTH):
                ch(nc.vector.tensor_scalar(lam_neg[:, l:l + 1], lam_neg[:, l:l + 1], LAM0[l], None, ALU.subtract))
                ch(nc.vector.memset(lam_rest[:, l:l + 1], 1.0 - LAM0[l]))

        def dve_second(v):
            with v.Fori(0, DEPTH) as l:
                ch = Chain(v, "dve_chain2", l * CHAINED)
                v.sem_inc(sem("x_ready2"), 1)
                v.wait_ge(sem("ssq_ready2"), l + 1)
                ch(nc.vector.tensor_scalar(ssq4, ssq4, 1.0 / D, None, ALU.mult))
                inverse_root2(v, ch, ssq4, 4, 1e-6, l * 2 + 1)
                v.wait_ge(sem("g_in"), (l + 1) * 32)
                for t in range(TT):
                    ch(nc.vector.scalar_tensor_tensor(mem_tm[:, t, :], mem_tm[:, t, :], ssq4[:, 2 + t:3 + t], g_m,
                                                      ALU.mult, ALU.mult))
                for t in range(TT):
                    ch(nc.vector.scalar_tensor_tensor(h_tm[:, t, :], x_tm[:, t, :], ssq4[:, t:t + 1], g_x, ALU.mult,
                                                      ALU.mult))
                v.sem_inc(sem("normed"), 1)
                job_n = 0

                def scale_max(kind, h, J):
                    if kind != "mem" and h == 0:
                        v.wait_ge(sem("bias_in"), (2 * l + (1 if kind == "diff" else 2)) * 32)
                    v.wait_ge(sem("s_full2"), l * NJOB + J + 1)
                    v.wait_ge(sem("turn_full"), l * NTURN + TURN0[(kind, h)])
                    G = MAPS[kind]
                    for m in range(G):
                        if kind == "mem":
                            ch(nc.vector.tensor_scalar(S3[:, m, :], ps[:, 2 + m, :], JOB_SCALE[kind], None, ALU.mult))
                        else:
                            b = bias[:, h if kind == "diff" else LH * m + h, :]
                            ch(nc.vector.scalar_tensor_tensor(S3[:, m, :], ps[:, 2 + m, :], JOB_SCALE[kind], b,
                                                              ALU.mult, ALU.add))
                    v.sem_inc(sem("s_taken2"), 1)
                    if kind == "diff":
                        ch(nc.vector.tensor_reduce(nmx3, S3[:, 0:2, :].rearrange("p m (t k) -> p (m t) k", t=TT), X,
                                                   ALU.max, negate=True))
                    elif kind == "dil":
                        ch(nc.vector.tensor_reduce(nmx3[:, 0:TT], S3.rearrange("p m (t k) -> p t m k", t=TT),
                                                   mybir.AxisListType.XY, ALU.max, negate=True))
                    else:
                        ch(nc.vector.tensor_reduce(nmx3[:, 0:TT], S3[:, 0, :].rearrange("p (t k) -> p t k", t=TT), X,
                                                   ALU.max, negate=True))
                    v.sem_inc(sem("max_ready2"), 1)

                def weigh(kind, h, J):
                    v.wait_ge(sem("p_ready2"), l * NJOB + J + 1)
                    n = 4 if kind == "diff" else TT
                    ch(nc.vector.reciprocal(rden3[:, 0:n], den3[:, 0:n]))
                    if kind == "diff":
                        ch(nc.vector.tensor_scalar(rden3[:, 2:4], rden3[:, 2:4], lam_neg[:, bass.ds(l, 1)], None,
                                                   ALU.mult))
                        for t in range(TT):
                            p0, p1 = (S3[:, m, t * T:(t + 1) * T] for m in range(2))
                            ch(nc.vector.tensor_scalar(p0, p0, rden3[:, t:t + 1], None, ALU.mult))
                            ch(nc.vector.scalar_tensor_tensor(p0, p1, rden3[:, 2 + t:3 + t], p0, ALU.mult, ALU.add))
                        v.sem_inc(sem("w_ready2"), 1)

                def gated(kind, h, J):
                    v.wait_ge(sem("o_full2"), l * NJOB + J + 2)
                    g = gate_of[kind]
                    if kind == "diff":
                        v.wait_ge(sem("o_squared"), l * DH + h + 1)
                    for t in range(TT):
                        part = g[:, t, h * P:(h + 1) * P]
                        by = 0.5 if kind == "diff" else rden3[:, t:t + 1]
                        ch(nc.vector.scalar_tensor_tensor(part, ps[:, 7, t * P:(t + 1) * P], by, part, ALU.mult,
                                                          ALU.mult))
                    v.sem_inc(sem("o_taken2"), 1)
                    if kind == "diff" and h == DH - 1:
                        flat = ssq16.rearrange("p h t -> p (h t)")
                        ch(nc.vector.tensor_scalar(flat, flat, 1.0 / DV, None, ALU.mult))
                        inverse_root2(v, ch, flat, 16, 1e-6, l * 2 + 2)
                        ch(nc.vector.tensor_scalar(flat, flat, lam_rest[:, bass.ds(l, 1)], None, ALU.mult))
                        for t in range(TT):
                            part = dgt[:, t, :].rearrange("p (h d) -> p h d", h=DH)
                            ch(nc.vector.tensor_tensor(part, part, over(ssq16[:, :, t], 2, DV), ALU.mult))
                        v.sem_inc(sem("diff_ready2"), 1)
                    elif kind != "diff" and h == LH - 1:
                        for t in range(TT):
                            ch(nc.vector.tensor_scalar(g[:, t, :], g[:, t, :], 0.5, None, ALU.mult))
                        v.sem_inc(sem(f"{kind}_ready2"), 1)

                gate_n = [0]

                def take(i, half):
                    (name, c), n = PLAN[i][0], HALF0[i] + half
                    bank, taken = ps[:, n % 2, :], sem(f"bank_taken{n % 2}")
                    if name == "w_in" and c in (6, 7, 17, 19):
                        gate_n[0] += 1
                        v.wait_ge(sem("tanh_ready"), l * 8 + gate_n[0])
                        g = dgt[:, half, (c - 6) * CW:(c - 5) * CW] if c < 8 else (lgt if c == 17 else mgt)[:, half, :]
                        ch(nc.vector.scalar_tensor_tensor(g, g, 1.0, bank, ALU.add, ALU.mult))
                        v.sem_inc(taken, 1)
                    elif name.startswith("br_"):
                        if name == "br_diff":
                            t, cols = half, slice(c * CW, (c + 1) * CW)
                            if half == 0:
                                wait_taken(v, l, i - 1)
                                v.wait_ge(sem("turn_full"), l * NTURN + TURN0["diff"] + 4)
                        else:
                            t, cols = half // 2, slice((half % 2) * CW, (half % 2 + 1) * CW)
                            if half == 0:
                                wait_taken(v, l, chunk_of("w_in", 23 if name == "br_dil" else 25))
                        v.wait_ge(sem("bank_full"), products(l, n + 1))
                        g, m = gates[:, t, cols], merged[:, t, cols]
                        if name == "br_diff":
                            ch(nc.vector.scalar_tensor_tensor(m, g, 1.0, bank, ALU.add, ALU.mult))
                            v.sem_inc(taken, 1)
                        else:
                            ch(nc.vector.scalar_tensor_tensor(g, g, 1.0, bank, ALU.add, ALU.mult))
                            ch(nc.vector.tensor_tensor(m, m, g, ALU.add))
                            v.sem_inc(taken, 1)
                            if name == "br_mem" and half == 3:
                                v.sem_inc(sem("merged_ready2"), 1)
                    elif name == "w_out":
                        v.wait_ge(sem("bank_full"), products(l, n + 1))
                        part = x_tm[:, half, c * CW:(c + 1) * CW]
                        ch(nc.vector.scalar_tensor_tensor(part, bank, 0.5, part, ALU.mult, ALU.add))
                        v.sem_inc(taken, 1)

                for i, (chunk, job, after) in enumerate(PLAN):
                    if job:
                        scale_max(*job, job_n)
                        weigh(*job, job_n)
                    for half in range(HALVES[i]):
                        take(i, half)
                    if job:
                        gated(*job, job_n)
                        job_n += 1
                assert ch.n == CHAINED, ch.n

        def pool_second(pool):
            with pool.Fori(0, DEPTH) as l:
                if True:
                    pool.wait_ge(sem("x_ready2"), l + 1)
                    pool.sem_inc(sem("loads_begun"), 1)
                    pool.dma_start(mem_tm, a["mem"][0].rearrange("(t p) d -> p t d", p=P)).then_inc(sem("mem_in"), 16)
                    pool.dma_start(g_x, a["g_norm"][bass.ds(l, 1), :].rearrange("a d -> (a d)").partition_broadcast(P)
                                   ).then_inc(sem("g_in"), 16)
                    pool.dma_start(g_m, a["g_mem"][bass.ds(l, 1), :].rearrange("a d -> (a d)").partition_broadcast(P)
                                   ).then_inc(sem("g_in"), 16)
                    for part, (h0, nh) in enumerate(((0, DH), (DH, LG * LH))):
                        if part:
                            pool.wait_ge(sem("max_ready2"), l * NJOB + DH)
                            pool.sem_inc(sem("loads_begun"), 1)
                        for t in range(TT):
                            src = bass.AP(gap_bias.tensor, h0 * P * GAPS + T - 1 - t * P, [[GAPS - 1, P], [P * GAPS, nh], [1, T]])
                            pool.dma_start(bias[:, 0:nh, t * T:(t + 1) * T], src).then_inc(sem("bias_in"), 16)

        def expert_load(sp, layer, n, e, s, after=True):
            w = w_slots[s]
            if after:
                sp.wait_ge(sem(f"down{layer}"), n - RINGS + 3)
            n1 = KD * FE
            sp.dma_start(w[:, 0:n1], a["moe_w1"][layer, e].rearrange("(p k) f -> p (k f)", k=KD)).then_inc(
                sem(f"w_in{layer}_{s}"), 16)
            sp.dma_start(w[:, n1:2 * n1], a["moe_w3"][layer, e].rearrange("(p k) f -> p (k f)", k=KD)).then_inc(
                sem(f"w_in{layer}_{s}"), 16)
            sp.dma_start(w[:, 2 * n1:].rearrange("p (k f) -> p k f", k=FE // P),
                         a["moe_w2"][layer, e].rearrange("(k p) f -> p k f", p=P)).then_inc(
                sem(f"w_in{layer}_{s}"), 16)

        def load_ln(sp, layer, half, after, value):
            sp.wait_ge(after, value)
            for dst, src in ((gain, a["ln_g"]), (shift, a["ln_b"])):
                sp.dma_start(dst, src[layer, half].partition_broadcast(P)).then_inc(sem("ln_in"), 16)

        @block.sync
        def _(sp):
            sp.dma_start(x_tm, a["x"][0].rearrange("(t p) d -> p t d", p=P)).then_inc(sem("x_in"), 16)
            sp.dma_start(consts[:, :], a["small"]).then_inc(sem("const_in"), 16)
            sp.dma_start(rel_sb[0:BUCKETS, :], a["rel_bias"]).then_inc(sem("rel_in"), 16)
            sp.dma_start(S.rearrange("p a b -> p (a b)"), a["gap_consts"]).then_inc(sem("gap_in"), 16)
            sp.dma_start(win, a["mla_w_in"][0].rearrange("(p k) n -> p k n", k=KD)).then_inc(sem("win_in"), 16)
            sp.dma_start(pos_i[:, :], a["positions"][0].rearrange("(t p) -> p t", p=P),
                         allow_slow_non_contiguous=True).then_inc(sem("pos_in"), 16)
            sp.dma_start(qg, a["mla_q_norm"][0].partition_broadcast(P)).then_inc(sem("norm_in"), 16)
            sp.dma_start(kvg, a["mla_kv_norm"][0].partition_broadcast(P)).then_inc(sem("norm_in"), 16)
            sp.dma_start(wuq, a["mla_w_uq"][0].rearrange("(k p) n -> p k n", p=P)).then_inc(sem("wuq_in"), 16)
            sp.dma_start(wukv, a["mla_w_ukv"][0]).then_inc(sem("wukv_in"), 16)
            sp.dma_start(wo, a["mla_w_o"][0].rearrange("(k p) n -> p k n", p=P)).then_inc(sem("wo_in"), 16)
            for layer in range(DEPTH):
                if layer:
                    sp.wait_ge(sem("down0"), nsw * NE + 2)
                for s in range(RINGS):
                    if s == 2:
                        load_ln(sp, layer, 0, sem("gain_free"), 2 * layer + 1)
                        if layer == 1:
                            sp.wait_ge(sem("pool_free"), 1)
                            pw, pband, pb, psc = pool_places
                            sp.dma_start(pband, a["band"]).then_inc(sem("pool_in"), 16)
                            sp.dma_start(pw, a["pool_w"][0].rearrange("g (k p) n -> p g k n", p=P)).then_inc(
                                sem("pool_in"), 16)
                            for dst_, src_ in ((pb, a["pool_b"]), (psc, a["pool_scale"])):
                                sp.dma_start(dst_, src_[0].partition_broadcast(P)).then_inc(sem("pool_in"), 16)
                    if s < 2 or layer == 1:
                        expert_load(sp, layer, s, s, s, False)
                    elif s == 2:
                        sp.wait_ge(sem("ln_done"), 1)
                        sp.dma_start(wr[:, :, 0:NG], a["moe_w_grp"][0].rearrange("(p k) n -> p k n", k=KD)).then_inc(
                            sem("route_in"), 16)
                        sp.dma_start(wr[:, :, NG:], a["moe_w_exp"][0].rearrange("(p k) n -> p k n", k=KD)).then_inc(
                            sem("route_in"), 16)
                        for c0, src_ in ((0, a["moe_b_grp"]), (NG, a["moe_b_exp"])):
                            sp.dma_start(br[:, c0:c0 + src_.shape[1]], src_[0].partition_broadcast(P)).then_inc(
                                sem("route_in"), 16)
                        expert_load(sp, layer, s, s, s, False)
                    else:
                        expert_load(sp, layer, s, s, s, False)
                if layer == 1:
                    sp.wait_ge(sem("ln_done"), 3)
                    sp.dma_start(wr[:, :, 0:NG], a["moe_w_grp"][1].rearrange("(p k) n -> p k n", k=KD)).then_inc(
                        sem("route_in"), 16)
                    sp.dma_start(wr[:, :, NG:], a["moe_w_exp"][1].rearrange("(p k) n -> p k n", k=KD)).then_inc(
                        sem("route_in"), 16)
                    for c0, src_ in ((0, a["moe_b_grp"]), (NG, a["moe_b_exp"])):
                        sp.dma_start(br[:, c0:c0 + src_.shape[1]], src_[1].partition_broadcast(P)).then_inc(
                            sem("route_in"), 16)
                load_ln(sp, layer, 1, sem("gain_free"), 2 * layer + 2)
                with sp.Fori(1, NE // RINGS) as j:
                    for s in range(RINGS):
                        expert_load(sp, layer, j * RINGS + s, j * RINGS + s, s)
                sp.wait_ge(sem(f"routed{layer}"), 1)
                nsw = sp.value_load(nsw_i[0:1, 0:1], min_val=1, max_val=SWEEPS)
                with sp.If(nsw > 1):
                    with sp.Fori(1, nsw) as i:
                        with sp.Fori(0, NE // RINGS) as j:
                            for s in range(RINGS):
                                expert_load(sp, layer, i * NE + j * RINGS + s, j * RINGS + s, s)
                with sp.Else():
                    sp.nop()
                sp.wait_ge(sem(f"y_out{layer}"), nsw * (16 * NE))
                sp.dma_start(Ys, y_sorted[0:NS, :].rearrange("(k p) d -> p k d", p=P)).then_inc(sem("ys_in"), 16)
            sp.wait_ge(sem("down1"), nsw * NE + 2)
            sp.sem_inc(sem("ring_free"), 1)
            sp_second(sp)
            sp.wait_ge(sem("final_ready"), 1)
            sp.dma_start(out[0].rearrange("(t p) d -> p t d", p=P), x_tm).then_inc(sem("out_done"), 16)
            sp.wait_ge(sem("out_done"), 16)

        def transpose_x(pe, n):
            for k in range(KD):
                bank = 4 + k // 2 % 4
                for t in range(TT):
                    i = nc.tensor.transpose(ps[:, bank, (k % 2) * T + t * P:(k % 2) * T + (t + 1) * P],
                                            x_tm[:, t, k::KD], ident)
                if k % 2:
                    i.then_inc(sem("xT_ps"), 1)

        def pe_experts(pe, layer):
            wsem = [sem(f"w_in{layer}_{s}") for s in range(RINGS)]

            def up(n, s, r):
                pe.wait_ge(sem(f"xe_ready{layer}"), n + 1)
                pe.wait_ge(wsem[s], 48 * (r + 1))
                pe.wait_ge(sem(f"psA_free{layer}"), n + 1)
                w = w_slots[s]
                for k in range(KD):
                    for g in range(4):
                        c0 = (g // 2) * KD * FE + k * FE + (g % 2) * P
                        i = nc.tensor.matmul(ps[SL * g:SL * g + SL, s % 2, 0:P], xe[:, s % 2, k * SL:(k + 1) * SL],
                                             w[:, c0:c0 + P], start=(k == 0), stop=(k == KD - 1),
                                             skip_group_check=True)
                i.then_inc(sem(f"up{layer}"), 1)

            def turn(n, s):
                pe.wait_ge(sem(f"hA_ready{layer}"), n + 1)
                pe.wait_ge(sem(f"hT_ready{layer}"), n + 1)
                nc.tensor.transpose(ps[:, 2 + s % 2, 0:P], hA[:, s % 2, :], ident).then_inc(sem(f"turned{layer}"), 1)

            def down(n, s):
                pe.wait_ge(sem(f"hT_ready{layer}"), n + 3)
                pe.wait_ge(sem(f"psY_free{layer}"), n + 1)
                w = w_slots[s][:, 2 * KD * FE:]
                for k in range(FE // P):
                    for g in range(4):
                        i = nc.tensor.matmul(ps[SL * g:SL * g + SL, 4 + s % 2, 0:T],
                                             hT[:, s % 2, k * SL:(k + 1) * SL],
                                             w[:, k * D + g * T:k * D + (g + 1) * T], start=(k == 0),
                                             stop=(k == FE // P - 1), skip_group_check=True)
                i.then_inc(sem(f"down{layer}"), 1)

            pe.wait_ge(sem(f"routed{layer}"), 1)
            nsw = pe.value_load(nsw_i[0:1, 0:1], min_val=1, max_val=SWEEPS)
            J = NE // RINGS
            with pe.Fori(0, nsw) as i:
                up(i * NE, 0, i * J)
                with pe.Fori(0, J - 1) as j:
                    for s in range(RINGS):
                        n = i * NE + j * RINGS + s
                        turn(n, s)
                        up(n + 1, (s + 1) % RINGS, i * J + j + (s + 1) // RINGS)
                        down(n, s)
                for s in range(RINGS):
                    n = i * NE + (J - 1) * RINGS + s
                    turn(n, s)
                    if s < RINGS - 1:
                        up(n + 1, s + 1, i * J + J - 1)
                    down(n, s)

        def pe_route(pe, layer):
            pe.wait_ge(sem("xT_ready"), 4 * (layer + 2))
            pe.wait_ge(sem("route_in"), 64 * (layer + 1))
            for t in range(TT):
                for k in range(KD):
                    i = nc.tensor.matmul(ps[:, 0, t * 128:t * 128 + NG + NE], xT[:, k, t * P:(t + 1) * P], wr[:, k, :],
                                         start=(k == 0), stop=(k == KD - 1))
            i.then_inc(sem("logits"), 1)
            pe.wait_ge(sem("A_ready"), layer + 1)
            for t in range(TT):
                nc.tensor.matmul(ps[0:NE, 1, 0:P], A[:, t, :], ones, start=(t == 0), stop=(t == 1))
            for t in range(TT):
                i = nc.tensor.matmul(ps[:, 2, 0:NE], ones, A[:, t, :], start=(t == 0), stop=(t == 1))
            i.then_inc(sem("counted"), 1)
            pe.wait_ge(sem("cntT_ready"), layer + 1)
            nc.tensor.matmul(ps[:, 3, 0:NE], cntT[0:NE, :], before[0:NE, 0:NE], start=True, stop=True)
            for t in range(TT):
                o_ = ps[:, 4 + t, 0:NE]
                nc.tensor.matmul(o_, cntT[0:NE, :], before[0:NE, 0:NE], start=True, stop=False)
                if t:
                    nc.tensor.matmul(o_, ones, A[:, 0, :], start=False, stop=False)
                i = nc.tensor.matmul(o_, before, A[:, t, :], start=False, stop=True)
            i.then_inc(sem("ranked"), 1)
            pe.wait_ge(sem("P_ready"), layer + 1)
            for k in range(KD):
                if k >= 4:
                    pe.wait_ge(sem("xs_ready"), KD * layer + k - 3)
                for t in range(TT):
                    i = nc.tensor.matmul(ps[:, k % 4, :], x_tm[:, t, k::KD], Pm[:, t, :], start=(t == 0), stop=(t == 1))
                i.then_inc(sem("xs_ps"), 1)
            pe.wait_ge(sem("CT_ready"), layer + 1)
            for h in range(2):
                for c in range(2):
                    for t in range(TT):
                        s = 2 * h + c
                        i = nc.tensor.transpose(ps[:, 6 + h, c * T + t * P:c * T + (t + 1) * P],
                                                CT[:, t, s * P:(s + 1) * P], ident)
            i.then_inc(sem("C_ps"), 1)
            pe.wait_ge(sem("xs_ready"), KD * (layer + 1))
            pe.sem_inc(sem(f"up{layer}"), 2)
            pe.sem_inc(sem(f"turned{layer}"), 2)
            pe.sem_inc(sem(f"down{layer}"), 2)

        def pe_combine(pe, layer):
            pe.wait_ge(sem("ys_in"), 16 * (layer + 1))
            pe.wait_ge(sem("C_ready"), layer + 1)
            for t in range(TT):
                for n in range(2):
                    for s in range(NS // P):
                        i = nc.tensor.matmul(ps[:, 2 * t + n, :], C[:, s, t * P:(t + 1) * P],
                                             Ys[:, s, n * 512:(n + 1) * 512], start=(s == 0), stop=(s == 3))
                    i.then_inc(sem("f_ps"), 1)

        @block.tensor
        def _(pe):
            pe.wait_ge(sem("x_in"), 16)
            pe.wait_ge(sem("const_in"), 16)
            transpose_x(pe, 0)
            pe.wait_ge(sem("rel_in"), 16)
            pe.wait_ge(sem("gap_in"), 16)
            nc.tensor.matmul(ps[0:BIASES, 3, :], rel_sb[0:BUCKETS, :], bias_onehot[0:BUCKETS, :], start=True,
                             stop=True).then_inc(sem("gap_ps"), 1)
            pe.wait_ge(sem("xT_ready"), 4)
            pe.wait_ge(sem("win_in"), 16)
            for t in range(TT):
                for k in range(KD):
                    i = nc.tensor.matmul(ps[:, t, 0:LAT], xT[:, k, t * P:(t + 1) * P], win[:, k, :],
                                         start=(k == 0), stop=(k == KD - 1))
            i.then_inc(sem("lat_ps"), 1)
            pe.wait_ge(sem("lat_normed"), 1)
            for c in range(3):
                for t in range(TT):
                    i = nc.tensor.transpose(ps[:, 2 + c // 2, (c % 2) * T + t * P:(c % 2) * T + (t + 1) * P],
                                            lat[:, t, c * P:(c + 1) * P], ident)
            i.then_inc(sem("cT_ps"), 1)
            pe.wait_ge(sem("cT_ready"), 1)
            pe.wait_ge(sem("wuq_in"), 16)
            pe.wait_ge(sem("wukv_in"), 16)
            m = 0
            for t in range(TT):
                for c in range(4):
                    if m >= 4:
                        pe.wait_ge(sem("q_ready"), m - 3)
                    for k in range(2):
                        i = nc.tensor.matmul(ps[:, 4 + m % 4, 0:4 * QH], cT[:, k, t * P:(t + 1) * P],
                                             wuq[:, k, c * 4 * QH:(c + 1) * 4 * QH], start=(k == 0), stop=(k == 1))
                    i.then_inc(sem("q_ps"), 1)
                    m += 1
            vw = wukv.rearrange("p (h c) -> p h c", c=NOPE + VD)
            for t in range(TT):
                for c in range(2):
                    i = nc.tensor.matmul(ps[:, 2 * t + c, :], cT[:, 2, t * P:(t + 1) * P],
                                         vw[:, 8 * c:8 * c + 8, NOPE:], start=True, stop=True)
                    i.then_inc(sem("v_ps"), 1)
            for c in range(8):
                if c < 4:
                    pe.wait_ge(sem("v_ready"), c + 1)
                else:
                    pe.wait_ge(sem("k_ready"), c - 3)
                for u in range(2):
                    h = 2 * c + u
                    i = nc.tensor.matmul(ps[0:NOPE, c % 4, u * T:(u + 1) * T], vw[:, h, 0:NOPE], cT[:, 2, :],
                                         start=True, stop=True)
                i.then_inc(sem("k_ps"), 1)
            pe.wait_ge(sem("q_ready"), 8)
            pe.wait_ge(sem("roped"), 1)
            for c in range(9):
                if c >= 4:
                    pe.wait_ge(sem("qT_ready"), c - 3)
                for u in range(2):
                    h = 2 * c + u
                    if h > NH:
                        continue
                    for t in range(TT):
                        i = nc.tensor.transpose(ps[0:QH, 4 + c % 4, u * T + t * P:u * T + (t + 1) * P],
                                                qtm[:, t, h, :], ident)
                i.then_inc(sem("qT_ps"), 1)
            pe.wait_ge(sem("k_ready"), 9)
            pe.wait_ge(sem("qT_ready"), 9)

            def scores(h):
                if h >= 2:
                    pe.wait_ge(sem("s_ready"), h - 1)
                for t in range(TT):
                    i = nc.tensor.matmul(ps[:, h % 2, t * T:(t + 1) * T], qT[0:QH, h, t * P:(t + 1) * P],
                                         kT[0:QH, h, :], start=True, stop=True)
                i.then_inc(sem("s_ps"), 1)

            def turn(h):
                pe.wait_ge(sem("p_ready"), h + 1)
                if h >= 2:
                    pe.wait_ge(sem("pT_ready"), h - 1)
                for k in range(2):
                    for t in range(TT):
                        i = nc.tensor.transpose(ps[:, 2 + h % 2, k * T + t * P:k * T + (t + 1) * P],
                                                S[:, h % 2, t * T + k * P:t * T + (k + 1) * P], ident)
                i.then_inc(sem("pT_ps"), 1)

            def values(h):
                pe.wait_ge(sem("pT_ready"), h + 1)
                if h >= 2:
                    pe.wait_ge(sem("o_ready"), h - 1)
                for t in range(TT):
                    for k in range(2):
                        i = nc.tensor.matmul(ps[:, 4 + h % 2, t * VD:(t + 1) * VD],
                                             PT[:, h % 2, k * T + t * P:k * T + (t + 1) * P],
                                             v_tm[:, k, h * VD:(h + 1) * VD], start=(k == 0), stop=(k == 1))
                i.then_inc(sem("o_ps"), 1)

            scores(0)
            for h in range(NH + 1):
                if h + 1 < NH:
                    scores(h + 1)
                if h < NH:
                    turn(h)
                if h >= 1:
                    values(h - 1)
            pe.wait_ge(sem("o_ready"), NH)
            for c in range(4):
                for u in range(2):
                    for t in range(TT):
                        k = 2 * c + u
                        i = nc.tensor.transpose(ps[:, c, u * T + t * P:u * T + (t + 1) * P],
                                                o_tm[:, t, k * P:(k + 1) * P], ident)
                i.then_inc(sem("oT_ps"), 1)
            pe.wait_ge(sem("oT_ready"), 4)
            pe.wait_ge(sem("wo_in"), 16)
            for t in range(TT):
                for n in range(2):
                    for k in range(KD):
                        i = nc.tensor.matmul(ps[:, 2 * t + n, :], o_T[:, k, t * P:(t + 1) * P],
                                             wo[:, k, n * 512:(n + 1) * 512], start=(k == 0), stop=(k == KD - 1))
                    i.then_inc(sem("f_ps"), 1)
            pe.wait_ge(sem("ln_done"), 1)
            transpose_x(pe, 1)
            pe_route(pe, 0)
            pe_experts(pe, 0)
            pe_combine(pe, 0)
            pw, pband, pb, psc = pool_places
            pe.wait_ge(sem("ln_done"), 2)
            pe.wait_ge(sem("pool_in"), 64)
            for c in range(4):
                for u in range(2):
                    k = 2 * c + u
                    for t in range(TT):
                        i = nc.tensor.matmul(ps[:, 4 + c, u * T:(u + 1) * T], x_tm[:, t, k * P:(k + 1) * P],
                                             pband[:, (c * TT + t) * T:(c * TT + t + 1) * T],
                                             start=(t == 0), stop=(t == 1))
                i.then_inc(sem("pool_ps"), 1)
            for t in range(TT):
                for n in range(2):
                    pe.wait_ge(sem("pool_ready"), 2 * n + 2)
                    for u in range(2):
                        g = 2 * n + u
                        for k in range(2):
                            i = nc.tensor.matmul(ps[:, 2 * t + n, u * PG:(u + 1) * PG],
                                                 xT[:, 2 * g + k, t * P:(t + 1) * P], pw[:, 2 * g + k, :],
                                                 start=(k == 0), stop=(k == 1))
                    i.then_inc(sem("f_ps"), 1)
            pe.wait_ge(sem("ln_done"), 3)
            transpose_x(pe, 3)
            pe_route(pe, 1)
            pe_experts(pe, 1)
            pe_combine(pe, 1)
            pe.sem_inc(sem("bank_full"), NHALF)
            pe.sem_inc(sem("o_full2"), 1)
            pe_second(pe)

        def act_experts(act, layer):
            act.wait_ge(sem(f"routed{layer}"), 1)
            nsw = act.value_load(nsw_i[0:1, 0:1], min_val=1, max_val=SWEEPS)
            act.sem_inc(sem(f"psA_free{layer}"), 2)
            act.sem_inc(sem(f"psY_free{layer}"), 2)

            def take_up(n, s):
                act.wait_ge(sem(f"up{layer}"), n + 3)
                act.wait_ge(sem(f"turned{layer}"), n + 1)
                nc.scalar.copy(hA[:, s % 2, :], ps[:, s % 2, 0:P]).then_inc(sem(f"hA_ready{layer}"), 1)
                act.wait_ge(sem(f"hA_ready{layer}"), n + 1)
                act.sem_inc(sem(f"psA_free{layer}"), 1)

            def silu(n, s):
                act.wait_ge(sem(f"turned{layer}"), n + 3)
                act.wait_ge(sem(f"hT_ready{layer}"), n + 1)
                nc.scalar.activation(sg[:, s % 2, :], ps[:, 2 + s % 2, 0:2 * SL], ACT.Silu).then_inc(
                    sem(f"silu{layer}"), 1)

            def take_y(n, s):
                act.wait_ge(sem(f"down{layer}"), n + 3)
                act.wait_ge(sem(f"yS_free{layer}"), n + 1)
                nc.scalar.copy(yS[:, s % 2, :], ps[:, 4 + s % 2, 0:T]).then_inc(sem(f"yS_ready{layer}"), 1)
                act.wait_ge(sem(f"yS_ready{layer}"), n + 1)
                act.sem_inc(sem(f"psY_free{layer}"), 1)

            J = NE // RINGS
            with act.Fori(0, nsw) as i:
                take_up(i * NE, 0)
                with act.Fori(0, J - 1) as j:
                    for s in range(RINGS):
                        n = i * NE + j * RINGS + s
                        silu(n, s)
                        take_up(n + 1, (s + 1) % RINGS)
                        take_y(n, s)
                for s in range(RINGS):
                    n = i * NE + (J - 1) * RINGS + s
                    silu(n, s)
                    if s < RINGS - 1:
                        take_up(n + 1, s + 1)
                    take_y(n, s)

        def act_root(act, k, n):
            act.wait_ge(sem("var_ready"), k)
            nc.scalar.activation(rt[:, 0:n], vare[:, 0:n], ACT.Sqrt).then_inc(sem("root_ready"), 1)

        def act_xT(act, n):
            for c in range(4):
                act.wait_ge(sem("xT_ps"), 4 * n + c + 1)
                nc.scalar.copy(xT[:, 2 * c:2 * c + 2, :], ps[:, 4 + c, :].rearrange("p (a b) -> p a b", a=2)).then_inc(
                    sem("xT_ready"), 1)

        def act_route(act, layer):
            act.wait_ge(sem("g_centred"), layer + 1)
            nc.scalar.activation(goh_e, geq, ACT.Exp).then_inc(sem("g_exp"), 1)
            act.wait_ge(sem("e_gap"), layer + 1)
            nc.scalar.activation(rat, tx, ACT.Exp).then_inc(sem("e_exp"), 1)
            for k in range(KD):
                act.wait_ge(sem("xs_ps"), KD * layer + k + 1)
                nc.scalar.copy(XsT[:, k, 0:NS], ps[:, k % 4, :]).then_inc(sem("xs_ready"), 1)
            act.wait_ge(sem("C_ps"), layer + 1)
            nc.scalar.copy(C, ps[:, 6:8, :].rearrange("p a (b c) -> p (a b) c", b=2)).then_inc(sem("C_ready"), 1)

        @block.scalar
        def _(act):
            act_xT(act, 0)
            act.wait_ge(sem("lat_sb"), 1)
            for t in range(TT):
                nc.scalar.activation(PT[:, t, 0:QL], lat[:, t, 0:QL], ACT.Square, accum_out=ssq[:, t, 0:1])
                i = nc.scalar.activation(PT[:, t, QL:QL + KVL], lat[:, t, QL:QL + KVL], ACT.Square,
                                         accum_out=ssq[:, t, 1:2])
            i.then_inc(sem("ssq"), 1)
            act_root(act, 1, 4)
            act.wait_ge(sem("angles"), 1)
            nc.scalar.activation(cs, rr, ACT.Sin).then_inc(sem("cs"), 1)
            act.wait_ge(sem("cT_ps"), 1)
            nc.scalar.copy(cT[:, 0:2, :], ps[:, 2, :].rearrange("p (a b) -> p a b", a=2))
            nc.scalar.copy(cT[:, 2, :], ps[:, 3, 0:T]).then_inc(sem("cT_ready"), 1)
            for t in range(TT):
                for c in range(2):
                    act.wait_ge(sem("v_ps"), 2 * t + c + 1)
                    nc.scalar.copy(v_tm[:, t, c * 512:(c + 1) * 512], ps[:, 2 * t + c, :]).then_inc(sem("v_ready"), 1)
            for c in range(8):
                act.wait_ge(sem("k_ps"), c + 1)
                nc.scalar.copy(kT[0:NOPE, 2 * c:2 * c + 2, :],
                               ps[0:NOPE, c % 4, :].rearrange("p (a b) -> p a b", a=2)).then_inc(sem("k_ready"), 1)
            for c in range(8):
                act.wait_ge(sem("qT_ps"), c + 1)
                nc.scalar.copy(qT[0:QH, 2 * c:2 * c + 2, :],
                               ps[0:QH, 4 + c % 4, :].rearrange("p (a b) -> p a b", a=2)).then_inc(sem("qT_ready"), 1)
            act.wait_ge(sem("qT_ps"), 9)
            nc.scalar.copy(kT[NOPE:QH, :, :], over(ps[NOPE:QH, 4, 0:T], 1, NH)).then_inc(sem("k_ready"), 1)
            act.sem_inc(sem("qT_ready"), 1)

            def exps(h):
                act.wait_ge(sem("max_ready"), h + 1)
                if h >= 2:
                    act.wait_ge(sem("den_free"), h - 1)
                for t in range(TT):
                    part = S[:, h % 2, t * T:(t + 1) * T]
                    i = nc.scalar.activation(part, part, ACT.Exp, bias=nmx[:, h % 2, t:t + 1],
                                             accum_out=den[:, h % 2, t:t + 1])
                i.then_inc(sem("p_ready"), 1)

            def take_pT(h):
                act.wait_ge(sem("pT_ps"), h + 1)
                if h >= 2:
                    act.wait_ge(sem("o_ps"), h - 1)
                nc.scalar.copy(PT[:, h % 2, :], ps[:, 2 + h % 2, :]).then_inc(sem("pT_ready"), 1)

            exps(0)
            for h in range(NH):
                if h + 1 < NH:
                    exps(h + 1)
                take_pT(h)
            for c in range(4):
                act.wait_ge(sem("oT_ps"), c + 1)
                nc.scalar.copy(o_T[:, 2 * c:2 * c + 2, :], ps[:, c, :].rearrange("p (a b) -> p a b", a=2)).then_inc(
                    sem("oT_ready"), 1)
            act_root(act, 2, TT)
            act_xT(act, 1)
            act_route(act, 0)
            act_experts(act, 0)
            act_root(act, 3, TT)
            for c in range(4):
                act.wait_ge(sem("pool_ps"), c + 1)
                nc.scalar.copy(xT[:, 2 * c:2 * c + 2, :], ps[:, 4 + c, :].rearrange("p (a b) -> p a b", a=2)).then_inc(
                    sem("pool_ready"), 1)
            act_root(act, 4, TT)
            act_xT(act, 2)
            act_route(act, 1)
            act_experts(act, 1)
            act_root(act, 5, TT)
            act.wait_ge(sem("lam_dots"), 1)
            nc.scalar.activation(lam_exp, lam_dot, ACT.Exp).then_inc(sem("lam_exps"), 1)
            act.sem_inc(sem("turn_taken"), 2)
            act.sem_inc(sem("bank_taken0"), 1)
            act.sem_inc(sem("bank_taken1"), 1)
            act_second(act)
            act.wait_ge(sem("x_ready2"), DEPTH + 1)
            for t in range(TT):
                i = nc.scalar.activation(PT3.rearrange("p a b -> p (a b)")[:, 0:D], x_tm[:, t, :], ACT.Square,
                                         accum_out=ssq4[:, t:t + 1])
                i.then_inc(sem("ssq_each"), 1)
                act.wait_ge(sem("ssq_each"), 4 * DEPTH + t + 1)
            act.sem_inc(sem("ssq_ready2"), 1)
            act_root2(act, 2 * DEPTH + 1, TT)

        roots = [0]

        def inverse_root(v, ch, var, n, eps):
            ch(nc.vector.tensor_scalar(vare[:, 0:n], var, eps, None, ALU.add))
            v.sem_inc(sem("var_ready"), 1)
            roots[0] += 1
            v.wait_ge(sem("root_ready"), roots[0])
            ch(nc.vector.reciprocal(rt[:, 0:n], rt[:, 0:n]))
            ch(nc.vector.tensor_tensor(rt2[:, 0:n], rt[:, 0:n], rt[:, 0:n], ALU.mult))
            ch(nc.vector.tensor_tensor(rt2[:, 0:n], rt2[:, 0:n], vare[:, 0:n], ALU.mult))
            ch(nc.vector.tensor_scalar(rt2[:, 0:n], rt2[:, 0:n], -0.5, 1.5, ALU.mult, ALU.add))
            ch(nc.vector.tensor_tensor(var, rt[:, 0:n], rt2[:, 0:n], ALU.mult))

        def layer_norm(v, ch, n, f_of):
            for t in range(TT):
                for h in range(2):
                    f = f_of(t, h)
                    part = x_tm[:, t, h * 512:(h + 1) * 512]
                    ch(nc.vector.scalar_tensor_tensor(part, part, ALPHA, f, ALU.mult, ALU.add))
                    ch(nc.vector.bn_stats(stats[:, t, 6 * h:6 * h + 6], part))
                ch(nc.vector.bn_aggr(agg[:, t, :], stats[:, t, :].rearrange("p (a b) -> p a b", a=2)))
            v.sem_inc(sem("f_taken"), 1)
            inverse_root(v, ch, agg[:, :, 1], TT, 1e-5)
            v.wait_ge(sem("ln_in"), 32 * (n + 1))
            for t in range(TT):
                ch(nc.vector.tensor_scalar(x_tm[:, t, :], x_tm[:, t, :], agg[:, t, 0:1], agg[:, t, 1:2],
                                           ALU.subtract, ALU.mult))
                ch(nc.vector.tensor_tensor(x_tm[:, t, :], x_tm[:, t, :], gain, ALU.mult))
                ch(nc.vector.tensor_tensor(x_tm[:, t, :], x_tm[:, t, :], shift, ALU.add))
            v.sem_inc(sem("ln_done"), 1)
            v.sem_inc(sem("gain_free"), 1)

        def first_max(ch, onehot, vals, mx, spare, spare1):
            ch(nc.vector.tensor_reduce(mx, vals, X, ALU.max))
            ch(nc.vector.tensor_tensor(spare, vals, over(mx, 2, 8), ALU.is_equal))
            ch(nc.vector.tensor_tensor(spare, spare, over(falling, 1, TT), ALU.mult))
            ch(nc.vector.tensor_reduce(spare1, spare, X, ALU.max))
            ch(nc.vector.tensor_tensor(onehot, spare, over(spare1, 2, 8), ALU.is_equal))

        def dve_route(v, ch, layer):
            v.wait_ge(sem("logits"), layer + 1)
            v.wait_ge(sem("route_in"), 64 * (layer + 1))
            for t in range(TT):
                ch(nc.vector.tensor_tensor(lg[:, t, :], ps[:, 0, t * 128:t * 128 + NG + NE], br, ALU.add))
            first_max(ch, goh, lg[:, :, 0:NG], gm, geq, gx)
            ch(nc.vector.tensor_tensor(geq, lg[:, :, 0:NG], over(gm, 2, 8), ALU.subtract))
            v.sem_inc(sem("g_centred"), 1)
            for t in range(TT):
                ch(nc.vector.tensor_tensor(tmp[:, t, 0:NE].rearrange("p (g j) -> p g j", g=NG),
                                           lg[:, t, NG:].rearrange("p (g j) -> p g j", g=NG),
                                           over(goh[:, t, :], 2, EG), ALU.mult))
                ch(nc.vector.tensor_reduce(es[:, t, :], tmp[:, t, 0:NE].rearrange("p (g j) -> p j g", g=NG), X, ALU.add))
            first_max(ch, o1, es, m1, eeq, gx)
            ch(nc.vector.scalar_tensor_tensor(es, o1, NEG, es, ALU.mult, ALU.add))
            first_max(ch, o2, es, m2, eeq, gx)
            ch(nc.vector.tensor_tensor(tx, m2, m1, ALU.subtract))
            v.sem_inc(sem("e_gap"), 1)
            for t in range(TT):
                for E, oh in ((E1, o1), (E2, o2)):
                    ch(nc.vector.tensor_tensor(E[:, t, :].rearrange("p (g j) -> p g j", g=NG),
                                               over(goh[:, t, :], 2, EG), over(oh[:, t, :], 1, NG), ALU.mult))
            ch(nc.vector.tensor_tensor(A, E1, E2, ALU.add))
            v.sem_inc(sem("A_ready"), 1)
            v.wait_ge(sem("g_exp"), layer + 1)
            ch(nc.vector.tensor_reduce(gs, goh_e, X, ALU.add))
            v.wait_ge(sem("e_exp"), layer + 1)
            ch(nc.vector.tensor_scalar(dn, rat, 1.0, None, ALU.add))
            ch(nc.vector.tensor_tensor(dn, dn, gs, ALU.mult))
            ch(nc.vector.reciprocal(g1, dn))
            ch(nc.vector.tensor_tensor(g2, rat, g1, ALU.mult))
            v.wait_ge(sem("counted"), layer + 1)
            ch(nc.vector.tensor_copy(cntT[0:NE, :], ps[0:NE, 1, 0:P]))
            v.sem_inc(sem("cntT_ready"), 1)
            ch(nc.vector.tensor_reduce(cmax[0:1, :], ps[0:1, 2, 0:NE], X, ALU.max))
            ch(nc.vector.tensor_scalar(swf[0:1, :], sweep_floor[0:1, :], cmax[0:1, 0:1], None, ALU.is_lt))
            ch(nc.vector.tensor_reduce(nswf[0:1, :], swf[0:1, :], X, ALU.add))
            ch(nc.vector.tensor_copy(nsw_i[0:1, :], nswf[0:1, :]))
            v.wait_ge(sem("ranked"), layer + 1)
            ch(nc.vector.tensor_scalar(last[0:1, :], nswf[0:1, :], float(SL), float(-SL), ALU.mult, ALU.add))
            ch(nc.vector.tensor_scalar(swf[0:1, :], sweep_floor[0:1, :], -1.0, last[0:1, 0:1], ALU.mult, ALU.add))
            for i in range(SWEEPS):
                ch(nc.vector.tensor_scalar(stf[0:1, i * NE:(i + 1) * NE], ps[0:1, 3, 0:NE], swf[0:1, i:i + 1], float(NS),
                                           ALU.add, ALU.min))
            ch(nc.vector.tensor_copy(starts_i[0:1, :], stf[0:1, :]))
            v.sem_inc(sem(f"routed{layer}"), 1)
            for E, d in ((E1, d1), (E2, d2)):
                for t in range(TT):
                    ch(nc.vector.tensor_tensor(dst[:, t, :], E[:, t, :], ps[:, 4 + t, 0:NE], ALU.mult))
                ch(nc.vector.tensor_reduce(d, dst, X, ALU.add))
            for t in range(TT):
                ch(nc.vector.tensor_scalar(tmp[:, t, :], iota, d1[:, t:t + 1], None, ALU.is_equal))
                ch(nc.vector.scalar_tensor_tensor(Pm[:, t, :], iota, d2[:, t:t + 1], tmp[:, t, :], ALU.is_equal, ALU.add))
            ch(nc.vector.memset(XsT[:, :, NS:], 0.0))
            v.sem_inc(sem("P_ready"), 1)
            for t in range(TT):
                ch(nc.vector.tensor_scalar(tmp[:, t, :], iota, d1[:, t:t + 1], g1[:, t:t + 1], ALU.is_equal, ALU.mult))
                ch(nc.vector.tensor_scalar(CT[:, t, :], iota, d2[:, t:t + 1], g2[:, t:t + 1], ALU.is_equal, ALU.mult))
                ch(nc.vector.tensor_tensor(CT[:, t, :], CT[:, t, :], tmp[:, t, :], ALU.add))
            v.sem_inc(sem("CT_ready"), 1)

        def dve_experts(v, layer):
            v.wait_ge(sem("xs_ready"), KD * (layer + 1))
            nsw = v.value_load(nsw_i[0:1, 0:1], min_val=1, max_val=SWEEPS)
            v.sem_inc(sem(f"hT_ready{layer}"), 2)

            def slots(n, e, i, s):
                v.wait_ge(sem(f"up{layer}"), n + 1)
                at = v.value_load(starts_i[0:1, bass.ds(i * NE + e, 1)], min_val=0, max_val=NS)
                nc.vector.tensor_copy(xe[:, s % 2, :].rearrange("p (k s) -> p k s", k=KD),
                                      XsT[:, :, bass.ds(at, SL)]).then_inc(sem(f"xe_ready{layer}"), 1)

            def gate(n, s):
                v.wait_ge(sem(f"silu{layer}"), n + 1)
                v.wait_ge(sem(f"down{layer}"), n + 1)
                nc.vector.tensor_tensor(hT[:, s % 2, :], sg[:, s % 2, :], ps[:, 2 + s % 2, 2 * SL:4 * SL],
                                        ALU.mult).then_inc(sem(f"hT_ready{layer}"), 1)

            J = NE // RINGS
            with v.Fori(0, nsw) as i:
                slots(i * NE, 0, i, 0)
                slots(i * NE + 1, 1, i, 1)
                with v.Fori(0, J - 1) as j:
                    for s in range(RINGS):
                        n = i * NE + j * RINGS + s
                        gate(n, s)
                        slots(n + 2, j * RINGS + s + 2, i, s)
                for s in range(RINGS):
                    n = i * NE + (J - 1) * RINGS + s
                    gate(n, s)
                    if s < 2:
                        slots(n + 2, (J - 1) * RINGS + s + 2, i, s)

        @block.vector
        def _(v):
            ch = Chain(v, "dve_chain")
            v.wait_ge(sem("pos_in"), 16)
            v.wait_ge(sem("const_in"), 16)
            v.wait_ge(sem("gap_ps"), 1)
            ch(nc.vector.tensor_tensor(bias_mask[0:BIASES, :], ps[0:BIASES, 3, :], bias_mask[0:BIASES, :], ALU.add))
            v.sem_inc(sem("gap_ready"), 1)
            ch(nc.vector.tensor_copy(posf, pos_i[:, :]))
            for t in range(TT):
                ch(nc.vector.tensor_scalar(ang[:, t, :], freq, posf[:, t:t + 1], None, ALU.mult))
            angf = ang.rearrange("p t f -> p (t f)")
            for c in range(2):
                k_, r_ = kk[:, c, :], rr[:, c, :]
                ch(nc.vector.tensor_scalar(k_, angf, float(1 / TWO_PI), 0.25 * c, ALU.mult, ALU.add))
                ch(nc.vector.tensor_scalar(k_, k_, ROUND, ROUND, ALU.add, ALU.subtract))
                ch(nc.vector.scalar_tensor_tensor(r_, k_, -PI_A, angf, ALU.mult, ALU.add))
                ch(nc.vector.scalar_tensor_tensor(r_, k_, -PI_B, r_, ALU.mult, ALU.add))
                ch(nc.vector.scalar_tensor_tensor(r_, k_, -PI_C, r_, ALU.mult, ALU.add))
                ch(nc.vector.tensor_scalar(r_, r_, float(c * np.pi / 2), 3.1415925, ALU.add, ALU.min))
                ch(nc.vector.tensor_scalar(r_, r_, -3.1415925, None, ALU.max))
            v.sem_inc(sem("angles"), 1)
            v.wait_ge(sem("lat_ps"), 1)
            ch(nc.vector.tensor_copy(lat, ps[:, 0:2, 0:LAT]))
            v.sem_inc(sem("lat_sb"), 1)
            ch(nc.vector.memset(qtm[:, :, NH, 0:NOPE], 0.0))
            ch(nc.vector.tensor_copy(qtm[:, :, NH, NOPE:], lat[:, :, QL + KVL:]))
            v.wait_ge(sem("ssq"), 1)
            v.wait_ge(sem("norm_in"), 32)
            for c, w in enumerate((QL, KVL)):
                ch(nc.vector.tensor_scalar(ssq[:, :, c], ssq[:, :, c], 1.0 / w, None, ALU.mult))
            inverse_root(v, ch, ssq.rearrange("p t c -> p (t c)"), 4, 1e-6)
            for c, (w, g, c0) in enumerate(((QL, qg, 0), (KVL, kvg, QL))):
                for t in range(TT):
                    part = lat[:, t, c0:c0 + w]
                    ch(nc.vector.scalar_tensor_tensor(part, part, ssq[:, t, c:c + 1], g, ALU.mult, ALU.mult))
            v.sem_inc(sem("lat_normed"), 1)
            m = 0
            for t in range(TT):
                for c in range(4):
                    v.wait_ge(sem("q_ps"), m + 1)
                    nc.vector.tensor_copy(qtm[:, t, 4 * c:4 * c + 4, :],
                                          ps[:, 4 + m % 4, 0:4 * QH].rearrange("p (a b) -> p a b", a=4)).then_inc(
                        sem("q_ready"), 1)
                    m += 1
            v.wait_ge(sem("q_ready"), 8)
            v.wait_ge(sem("cs"), 1)
            H1 = NH + 1
            for t in range(TT):
                x1, x2 = qtm[:, t, :, NOPE:NOPE + RH], qtm[:, t, :, NOPE + RH:]
                sn = over(cs[:, 0, t * RH:(t + 1) * RH], 1, H1)
                co = over(cs[:, 1, t * RH:(t + 1) * RH], 1, H1)
                f = [rope_tmp[:, i, :].rearrange("p (h r) -> p h r", h=H1) for i in range(4)]
                ch(nc.vector.tensor_tensor(f[0], x1, co, ALU.mult))
                ch(nc.vector.tensor_tensor(f[1], x2, sn, ALU.mult))
                ch(nc.vector.tensor_tensor(f[2], x2, co, ALU.mult))
                ch(nc.vector.tensor_tensor(f[3], x1, sn, ALU.mult))
                ch(nc.vector.tensor_tensor(x1, f[0], f[1], ALU.subtract))
                ch(nc.vector.tensor_tensor(x2, f[2], f[3], ALU.add))
            v.sem_inc(sem("roped"), 1)

            def mask(h):
                v.wait_ge(sem("s_ps"), h + 1)
                if h >= 2:
                    v.wait_ge(sem("pT_ps"), h - 1)
                nc.vector.scalar_tensor_tensor(S[:, h % 2, :], ps[:, h % 2, :], MLA_SCALE, causal, ALU.mult,
                                               ALU.add).then_inc(sem("s_ready"), 1)
                v.wait_ge(sem("s_ready"), h + 1)
                nc.vector.tensor_reduce(nmx[:, h % 2, :], S[:, h % 2, :].rearrange("p (t k) -> p t k", t=TT), X,
                                        ALU.max, negate=True).then_inc(sem("max_ready"), 1)

            def norm_o(h):
                v.wait_ge(sem("p_ready"), h + 1)
                ch(nc.vector.reciprocal(rden[:, h % 2, :], den[:, h % 2, :]))
                v.sem_inc(sem("den_free"), 1)
                v.wait_ge(sem("o_ps"), h + 1)
                for t in range(TT):
                    i = nc.vector.tensor_scalar(o_tm[:, t, h * VD:(h + 1) * VD], ps[:, 4 + h % 2, t * VD:(t + 1) * VD],
                                                rden[:, h % 2, t:t + 1], None, ALU.mult)
                i.then_inc(sem("o_ready"), 1)

            v.wait_ge(sem("gap_out"), 16)
            mask(0)
            for h in range(NH + 1):
                if h + 1 < NH:
                    mask(h + 1)
                if h >= 1:
                    norm_o(h - 1)
            v.sem_inc(sem("gain_free"), 1)
            v.wait_ge(sem("f_ps"), 4)
            layer_norm(v, ch, 0, lambda t, h: ps[:, 2 * t + h, :])
            dve_route(v, ch, 0)
            dve_experts(v, 0)
            v.wait_ge(sem("f_ps"), 8)
            v.sem_inc(sem("pool_free"), 1)
            layer_norm(v, ch, 1, lambda t, h: ps[:, 2 * t + h, :])
            pw, pband, pb, psc = pool_places
            v.wait_ge(sem("f_ps"), 12)
            for t in range(TT):
                for n in range(2):
                    c0 = slice(n * 512, (n + 1) * 512)
                    ch(nc.vector.tensor_tensor(pool_y[:, t, c0], ps[:, 2 * t + n, :], pb[:, c0], ALU.add))
                    ch(nc.vector.tensor_tensor(pool_y[:, t, c0], pool_y[:, t, c0], psc[:, c0], ALU.mult))
            layer_norm(v, ch, 2, lambda t, h: pool_y[:, t, h * 512:(h + 1) * 512])
            dve_route(v, ch, 1)
            dve_experts(v, 1)
            v.wait_ge(sem("f_ps"), 16)
            layer_norm(v, ch, 3, lambda t, h: ps[:, 2 * t + h, :])
            dve_lambda(v, ch)
            v.sem_inc(sem("s_taken2"), 1)
            v.sem_inc(sem("o_taken2"), 1)
            dve_second(v)
            v.sem_inc(sem("x_ready2"), 1)
            v.wait_ge(sem("ssq_ready2"), DEPTH + 1)
            ch(nc.vector.tensor_scalar(ssq4[:, 0:TT], ssq4[:, 0:TT], 1.0 / D, None, ALU.mult))
            inverse_root2(v, ch, ssq4[:, 0:TT], TT, 1e-6, 2 * DEPTH + 1)
            v.wait_ge(sem("gf_in"), 16)
            for t in range(TT):
                ch(nc.vector.scalar_tensor_tensor(x_tm[:, t, :], x_tm[:, t, :], ssq4[:, t:t + 1], g_x, ALU.mult,
                                                  ALU.mult))
            v.sem_inc(sem("final_ready"), 1)

        def pool_experts(pool, layer):
            pool.wait_ge(sem(f"routed{layer}"), 1)
            nsw = pool.value_load(nsw_i[0:1, 0:1], min_val=1, max_val=SWEEPS)
            pool.sem_inc(sem(f"yS_free{layer}"), 2)
            with pool.Fori(0, nsw) as i:
                with pool.Fori(0, NE // 2) as j:
                    for s in range(2):
                        n = i * NE + j * 2 + s
                        at = pool.value_load(starts_i[0:1, bass.ds(i * NE + j * 2 + s, 1)], min_val=0, max_val=NS)
                        pool.wait_ge(sem(f"yS_ready{layer}"), n + 1)
                        pool.dma_start(y_sorted[bass.ds(at, SL), :].rearrange("s (g c) -> g s c", g=4),
                                       yS[:, s % 2, :]).then_inc(sem(f"y_out{layer}"), 16)
                        pool.wait_ge(sem(f"y_out{layer}"), (n + 1) * 16)
                        pool.sem_inc(sem(f"yS_free{layer}"), 1)

        @block.gpsimd
        def _(pool):
            pool.wait_ge(sem("gap_ready"), 1)
            pool.dma_start(gap_bias, over(bias_mask[0:BIASES, :], 1, P)).then_inc(sem("gap_out"), 16)
            pool_experts(pool, 0)
            pool_experts(pool, 1)
            pool.wait_ge(sem("ln_done"), 4)
            pool.dma_start(lam_in.rearrange("p a b -> p (a b)"),
                           a["diff_lambda"].rearrange("l a d -> (l a d)").partition_broadcast(P)).then_inc(
                sem("lam_in"), 16)
            pool.wait_ge(sem("gap_out"), 16)
            pool_second(pool)
            pool.wait_ge(sem("x_ready2"), DEPTH + 1)
            pool.dma_start(g_x, a["g_final"].partition_broadcast(P)).then_inc(sem("gf_in"), 16)


_INS = ['x', 'positions', 'ln_g', 'ln_b', 'mla_w_in', 'mla_q_norm', 'mla_w_uq', 'mla_kv_norm', 'mla_w_ukv', 'mla_w_o',
        'pool_w', 'pool_b', 'pool_scale', 'moe_w_grp', 'moe_b_grp', 'moe_w_exp', 'moe_b_exp', 'moe_w1', 'moe_w3',
        'moe_w2']

_INS2 = ['mem', 'g_norm', 'w_in', 'diff_lambda', 'w_mem_kv', 'g_mem', 'w_br_diff', 'w_br_dil', 'w_br_mem', 'w_out',
         'rel_bias', 'g_final']


def kernel(**inputs):
    import numpy as _np
    import concourse.bacc as _bacc
    from concourse import mybir as _mybir
    from concourse.bass_utils import run_bass_kernel_spmd as _run

    nc = _bacc.Bacc("TRN2", target_bir_lowering=False, num_devices=1)
    arrays, args = {}, {}

    def give(name, a):
        a = _np.ascontiguousarray(a)
        arrays[f"in_{name}_dram"] = a
        args[name] = nc.dram_tensor(f"in_{name}_dram", a.shape, _mybir.dt.from_np(a.dtype), kind="ExternalInput").ap()

    for name in _INS:
        give(name, inputs[name])
    for name in _INS2:
        give(name, inputs[name + '_2'])
    give('gap_consts', bias_constants())
    small, band = shape_constants()
    give("small", small)
    give("band", band)
    res = nc.dram_tensor("out_0_dram", (1, T, D), _mybir.dt.float32, kind="ExternalOutput").ap()
    build(nc, args, res)
    r = _run(nc, [arrays], core_ids=[0])
    return r.results[0]["out_0_dram"]
```
